# Optimizing a Trainium2 kernel written in Bass

```python
import math
import jax, jax.numpy as jnp
from jax import lax
import numpy as np

D_MODEL = 1024
BATCH = 1
SEQ = 512
DEPTH = 2

N_META = 16
CHUNK = 128
Q_BLOCK = 128
CONV_W = 256
CONV_K = 3
RET_HEADS = 4
RET_DK = 64
RET_DV = 64
MLA_HEADS = 8
MLA_NOPE = 64
MLA_ROPE = 32
MLA_V = 64
MLA_QK = MLA_NOPE + MLA_ROPE
Q_LORA = 256
KV_LORA = 128
MIX_OUT = CONV_W + RET_HEADS * RET_DV + MLA_HEADS * MLA_V
D_FF = 4 * D_MODEL
ROPE_BASE = 10000.0
NORM_EPS = 1e-6
IN_SIZES = (CONV_W, CONV_W, CONV_W,
            RET_HEADS * RET_DK, RET_HEADS * RET_DK, RET_HEADS * RET_DV, RET_HEADS * RET_DV,
            Q_LORA, KV_LORA, MLA_ROPE)
D_IN = sum(IN_SIZES)

kernel_name = "hymba_conv_retention_mla_hybrid"

def rms_norm(x, g):
    xf = x.astype(jnp.float32)
    y = xf * lax.rsqrt(jnp.mean(jnp.square(xf), axis=-1, keepdims=True) + NORM_EPS)
    return (y * g.astype(jnp.float32)).astype(x.dtype)

def rope_tables(n_pos, dim, dtype):
    inv = 1.0 / (ROPE_BASE ** (jnp.arange(0, dim, 2, dtype=jnp.float32) / dim))
    ang = jnp.arange(n_pos, dtype=jnp.float32)[:, None] * inv[None, :]
    return jnp.cos(ang).astype(dtype), jnp.sin(ang).astype(dtype)

def apply_rope(x, cos, sin):
    x1, x2 = jnp.split(x, 2, axis=-1)
    c = cos[None, :, None, :]
    s = sin[None, :, None, :]
    return jnp.concatenate([x1 * c - x2 * s, x2 * c + x1 * s], axis=-1)

def causal_dwconv(u, w):
    return lax.conv_general_dilated(
        u, w[:, None, :].astype(u.dtype), window_strides=(1,), padding=[(CONV_K - 1, 0)],
        dimension_numbers=('NWC', 'WIO', 'NWC'), feature_group_count=u.shape[-1])

def chunkwise_retention(q, k, v):
    B, T, H, dk = q.shape
    dv = v.shape[-1]
    pad = CHUNK - N_META
    f32 = jnp.float32
    padw = ((0, 0), (pad, 0), (0, 0), (0, 0))
    qp = jnp.pad(q.astype(f32), padw)
    kp = jnp.pad(k.astype(f32), padw)
    vp = jnp.pad(v.astype(f32), padw)
    n = (T + pad) // CHUNK

    def to_chunks(a):
        return a.reshape(B, n, CHUNK, H, a.shape[-1]).transpose(1, 0, 3, 2, 4)

    log_g = jnp.log1p(-jnp.exp2(-5.0 - jnp.arange(H, dtype=f32)))
    idx = jnp.arange(CHUNK, dtype=f32)
    diff = idx[:, None] - idx[None, :]
    decay = jnp.where(diff >= 0, jnp.exp(jnp.maximum(diff, 0.0)[None] * log_g[:, None, None]), 0.0)
    xi = jnp.exp((idx[None, :] + 1.0) * log_g[:, None])[..., None]
    zeta = jnp.exp((CHUNK - 1.0 - idx[None, :]) * log_g[:, None])[..., None]
    chunk_decay = jnp.exp(CHUNK * log_g)[:, None, None]

    def step(state, xs):
        qc, kc, vc = xs
        scores = jnp.einsum('bhid,bhjd->bhij', qc, kc) * decay
        inner = jnp.einsum('bhij,bhje->bhie', scores, vc)
        cross = jnp.einsum('bhid,bhde->bhie', qc, state) * xi
        new_state = chunk_decay * state + jnp.einsum('bhjd,bhje->bhde', kc * zeta, vc)
        return new_state, inner + cross

    state0 = jnp.zeros((B, H, dk, dv), f32)
    _, out = lax.scan(step, state0, (to_chunks(qp), to_chunks(kp), to_chunks(vp)))
    out = out.transpose(1, 0, 3, 2, 4).reshape(B, n * CHUNK, H, dv)[:, pad:]
    return out.astype(q.dtype)

def block_causal_attention(q, k, v):
    T = q.shape[1]
    scale = 1.0 / math.sqrt(q.shape[-1])
    bounds = [(0, N_META)] + [(s, min(s + Q_BLOCK, T)) for s in range(N_META, T, Q_BLOCK)]
    outs = []
    for s, e in bounds:
        qb, kb, vb = q[:, s:e], k[:, :e], v[:, :e]
        logits = jnp.einsum('bqhd,bkhd->bhqk', qb, kb).astype(jnp.float32) * scale
        mask = jnp.arange(e)[None, :] <= jnp.arange(s, e)[:, None]
        p = jax.nn.softmax(jnp.where(mask, logits, -jnp.inf), axis=-1).astype(vb.dtype)
        outs.append(jnp.einsum('bhqk,bkhd->bqhd', p, vb))
    return jnp.concatenate(outs, axis=1)

def hybrid_layer(x, cos_r, sin_r, cos_m, sin_m, attn_norm_g, w_in, conv_w, ret_gn_g,
                 q_norm_g, w_uq, kv_norm_g, w_ukv, q_head_norm_g, k_head_norm_g, w_out,
                 mlp_norm_g, w_mlp_in, w_mlp_out):
    B, T, _ = x.shape
    h = rms_norm(x, attn_norm_g)
    proj = h @ w_in
    offs = []
    acc = 0
    for sz in IN_SIZES[:-1]:
        acc += sz
        offs.append(acc)
    cb, cc, ch, rq, rk, rv, rg, cq, ckv, kr = jnp.split(proj, offs, axis=-1)

    y_conv = cb * causal_dwconv(cc * ch, conv_w)

    q_r = apply_rope(rq.reshape(B, T, RET_HEADS, RET_DK), cos_r, sin_r)
    k_r = apply_rope(rk.reshape(B, T, RET_HEADS, RET_DK), cos_r, sin_r) * (RET_DK ** -0.5)
    v_r = rv.reshape(B, T, RET_HEADS, RET_DV)
    o_r = rms_norm(chunkwise_retention(q_r, k_r, v_r), ret_gn_g)
    y_ret = jax.nn.silu(rg) * o_r.reshape(B, T, RET_HEADS * RET_DV)

    q_m = (rms_norm(cq, q_norm_g) @ w_uq).reshape(B, T, MLA_HEADS, MLA_QK)
    kv = (rms_norm(ckv, kv_norm_g) @ w_ukv).reshape(B, T, MLA_HEADS, MLA_NOPE + MLA_V)
    k_nope, v_m = kv[..., :MLA_NOPE], kv[..., MLA_NOPE:]
    k_rope = jnp.broadcast_to(kr[:, :, None, :], (B, T, MLA_HEADS, MLA_ROPE))
    k_m = jnp.concatenate([k_nope, k_rope], axis=-1)
    q_m = rms_norm(q_m, q_head_norm_g)
    k_m = rms_norm(k_m, k_head_norm_g)
    q_m = jnp.concatenate([q_m[..., :MLA_NOPE], apply_rope(q_m[..., MLA_NOPE:], cos_m, sin_m)], axis=-1)
    k_m = jnp.concatenate([k_m[..., :MLA_NOPE], apply_rope(k_m[..., MLA_NOPE:], cos_m, sin_m)], axis=-1)
    y_mla = block_causal_attention(q_m, k_m, v_m).reshape(B, T, MLA_HEADS * MLA_V)

    x = x + jnp.concatenate([y_conv, y_ret, y_mla], axis=-1) @ w_out

    u = rms_norm(x, mlp_norm_g) @ w_mlp_in
    return x + jnp.square(jax.nn.relu(u)) @ w_mlp_out

def setup_inputs(seed: int = 0) -> dict:
    key = jax.random.key(seed)
    ks = jax.random.split(key, 16)
    nrm = jax.random.normal

    def gain(k, shape):
        return 1.0 + 0.02 * nrm(k, shape, jnp.float32)

    return {
        "x": nrm(ks[0], (BATCH, SEQ, D_MODEL), jnp.float32),
        "meta_tokens": nrm(ks[1], (N_META, D_MODEL), jnp.float32),
        "attn_norm_g": gain(ks[2], (DEPTH, D_MODEL)),
        "w_in": nrm(ks[3], (DEPTH, D_MODEL, D_IN), jnp.float32) * D_MODEL ** -0.5,
        "conv_w": nrm(ks[4], (DEPTH, CONV_K, CONV_W), jnp.float32) * CONV_K ** -0.5,
        "ret_gn_g": gain(ks[5], (DEPTH, RET_HEADS, RET_DV)),
        "q_norm_g": gain(ks[6], (DEPTH, Q_LORA)),
        "w_uq": nrm(ks[7], (DEPTH, Q_LORA, MLA_HEADS * MLA_QK), jnp.float32) * Q_LORA ** -0.5,
        "kv_norm_g": gain(ks[8], (DEPTH, KV_LORA)),
        "w_ukv": nrm(ks[9], (DEPTH, KV_LORA, MLA_HEADS * (MLA_NOPE + MLA_V)), jnp.float32) * KV_LORA ** -0.5,
        "q_head_norm_g": gain(ks[10], (DEPTH, MLA_QK)),
        "k_head_norm_g": gain(ks[11], (DEPTH, MLA_QK)),
        "w_out": nrm(ks[12], (DEPTH, MIX_OUT, D_MODEL), jnp.float32) * MIX_OUT ** -0.5,
        "mlp_norm_g": gain(ks[13], (DEPTH, D_MODEL)),
        "w_mlp_in": nrm(ks[14], (DEPTH, D_MODEL, D_FF), jnp.float32) * D_MODEL ** -0.5,
        "w_mlp_out": nrm(ks[15], (DEPTH, D_FF, D_MODEL), jnp.float32) * D_FF ** -0.5,
    }

def reference(x, meta_tokens, attn_norm_g, w_in, conv_w, ret_gn_g, q_norm_g, w_uq, kv_norm_g,
              w_ukv, q_head_norm_g, k_head_norm_g, w_out, mlp_norm_g, w_mlp_in, w_mlp_out):
    B = x.shape[0]
    meta = jnp.broadcast_to(meta_tokens.astype(x.dtype)[None], (B, N_META, D_MODEL))
    h = jnp.concatenate([meta, x], axis=1)
    T = h.shape[1]
    cos_r, sin_r = rope_tables(T, RET_DK, h.dtype)
    cos_m, sin_m = rope_tables(T, MLA_ROPE, h.dtype)
    for l in range(DEPTH):
        h = hybrid_layer(h, cos_r, sin_r, cos_m, sin_m, attn_norm_g[l], w_in[l], conv_w[l],
                         ret_gn_g[l], q_norm_g[l], w_uq[l], kv_norm_g[l], w_ukv[l],
                         q_head_norm_g[l], k_head_norm_g[l], w_out[l], mlp_norm_g[l],
                         w_mlp_in[l], w_mlp_out[l])
    return h[:, N_META:]


_drawn_inputs = setup_inputs


def setup_inputs(seed=0):
    import zlib

    import numpy as np

    out = dict(_drawn_inputs(seed))
    spreads = {}
    factors = {'ret_gn_g': 7.842,
     'q_norm_g': 8.0,
     'kv_norm_g': 8.0,
     'q_head_norm_g': 8.0,
     'k_head_norm_g': 8.0}
    for name, (base, spread) in spreads.items():
        noise = np.random.default_rng([zlib.crc32(name.encode()), seed]).standard_normal(out[name].shape)
        drawn = base * np.exp(spread * noise) if base else spread * noise
        out[name] = __import__('jax').numpy.asarray(drawn.astype(out[name].dtype))
    for name, factor in factors.items():
        out[name] = (out[name] * factor).astype(out[name].dtype)
    return out
```

```python
from contextlib import ExitStack

import concourse.bass as bass
from concourse import mybir

F32 = mybir.dt.float32
F32R = mybir.dt.float32r
BF16 = mybir.dt.bfloat16
ALU = mybir.AluOpType
ACT = mybir.ActivationFunctionType
AX = mybir.AxisListType.X

P = 128
DEPTH, D, SEQ, META = 2, 1024, 512, 16
T = META + SEQ
TH = T // 2
KT = D // P
EPS = 1e-6
CONV_W = 256
RH, RD = 4, 64
NH, NOPE, ROPE, DV = 8, 64, 32, 64
QK = NOPE + ROPE
HG = NH // 2
Q_LORA, KV_LORA = 256, 128
DFF = 4 * D
FG = 1024
NGRP = DFF // FG
NT = 5

OFF_B, OFF_C, OFF_H = 0, 256, 512
OFF_RQ, OFF_RK, OFF_RV, OFF_RG = 768, 1024, 1280, 1536
OFF_CQ, OFF_CKV = 1792, 2048
D_IN = 2208

TA = [(0, META)] + [(META + P * i, P) for i in range(NT - 1)]
TB = [(P * i, min(P, T - P * i)) for i in range(NT)]

N_IN, N_OUT = 18, 8
PRE_TILES = N_IN + N_OUT
GT = 16
L_TILES = PRE_TILES + GT * NGRP
PRE_HALVES = 32
L_HALVES = PRE_HALVES + GT * NGRP
PRE_BLOCKS = PRE_HALVES // 2
L_BLOCKS = L_HALVES // 2
WS = 4
SS = 2

HALVES = ([("T", n) for n in range(6)] + [("U", 0), ("U", 1)] + [("T", n) for n in range(6, 10)] + [("U", 2), ("U", 3)]
          + [("T", 10), ("T", 11)] + [("U", 4), ("U", 5)] + [("T", n) for n in range(12, PRE_TILES)])
TILE_HALF = {n: i for i, (kind, n) in enumerate(HALVES) if kind == "T"}
MLA_HALF = {n: i for i, (kind, n) in enumerate(HALVES) if kind == "U"}
SLOT = {}
for _n in range(PRE_TILES):
    SLOT[TILE_HALF[_n]] = _n % 4 if _n < 4 or _n >= 18 - 2 else _n % 2
for _n in range(18, PRE_TILES):
    SLOT[TILE_HALF[_n]] = (_n - 18) % 4
SLOT[TILE_HALF[16]], SLOT[TILE_HALF[17]] = 2, 3
for _n in range(6):
    SLOT[MLA_HALF[_n]] = 2 + _n % 2
LOADS = {0: [4], 1: [5], 2: [6], 3: [7], 4: [8], 5: [9], 6: [10], 7: [11, 12, 13], 8: [14], 9: [15, 16, 17],
         10: [18], 11: [19], 12: [20], 13: [21, 22, 23], 14: [24], 15: [25], 16: [26], 17: [27],
         18: [28], 19: [29], 20: [30], 21: [31]}
FREED = {4: ("T", 0), 5: ("T", 1), 6: ("T", 2), 7: ("T", 3), 8: ("T", 4), 9: ("T", 5), 10: ("T", 6), 11: ("T", 7),
         12: ("U", 4), 13: ("U", 4), 14: ("T", 8), 15: ("T", 9), 16: ("U", 9), 17: ("U", 9), 18: ("T", 10),
         19: ("T", 11), 20: ("T", 12), 21: ("T", 13), 22: ("U", 14), 23: ("U", 19), 24: ("T", 14), 25: ("T", 15),
         26: ("T", 16), 27: ("T", 17), 28: ("T", 18), 29: ("T", 19), 30: ("T", 20), 31: ("T", 21)}

GAPS = {n: [] for n in range(6, 15)}
_u = 0
_t = 0
for _gap, _cnt in zip(range(6, 15), [3, 2, 3, 2, 3, 2, 3, 2, 0]):
    GAPS[_gap] = [("tr", _t + _i) for _i in range(_u - _t)]
    _t = _u
    GAPS[_gap] += [("u", _u + _i) for _i in range(_cnt)]
    _u += _cnt
AUX_SEQ = [x for g in range(6, 15) for x in GAPS[g]]
AUX_BANK = {x: 4 + i % 4 for i, x in enumerate(AUX_SEQ)}
AUX_PREV = {x: (AUX_SEQ[i - 4] if i >= 4 else None) for i, x in enumerate(AUX_SEQ)}

CONSTS = {}
_c = 0
for _name, _w in (("ident", P), ("perm", P), ("ones", P), ("keep", P), ("rope_c", T), ("rope_s", T),
                  ("tok_c", NT * ROPE), ("tok_s", NT * ROPE), ("g_out", NT * RH), ("g_in", NT * RH),
                  ("eps", 1), ("eps_q", 1)):
    CONSTS[_name] = (_c, _w)
    _c += _w
N_CONST = _c
PARAMS = {}
_c = 0
for _name, _w in (("attn_g", KT), ("mlp_g", KT), ("qn_g", 2), ("kvn_g", 1), ("conv", 6), ("ret_g", 2),
                  ("qh_g", 1), ("kh_g", 1), ("qrope_g", ROPE), ("krope_g", ROPE)):
    PARAMS[_name] = (_c, _w)
    _c += _w
N_PARAM = _c
NEG = -1e30


def trunk(nc, x, meta, consts, maskneg, params, w_in, w_uq, w_ukv, w_out, w_mlp_in, w_mlp_out, out):
    with ExitStack() as ctx:
        at = [nc.sbuf_base + (-nc.sbuf_base) % 32]

        def own(name, shape, dt=F32):
            size = 4 if dt != BF16 else 2
            for s in shape[1:]:
                size *= s
            off = at[0]
            at[0] += size + (-size) % 32
            return nc.alloc_sbuf_tensor_at(name, shape, dt, offset=off), off

        def over(name, shape, off, dt=F32):
            return nc.alloc_sbuf_tensor_at(name, shape, dt, offset=off)

        def sem(name):
            return ctx.enter_context(nc.semaphore(name))

        TB4 = T * 4
        xT, _ = own("xT", [P, KT, T])
        hh, hreg = own("hh", [P, KT, T], F32R)
        hl, _ = own("hl", [P, KT, T], F32R)
        yh, yreg = own("yh", [P, KT, T], F32R)
        yl, _ = own("yl", [P, KT, T], F32R)
        stage, _ = own("stage", [P, SS, 2048])
        wh, _ = own("wh", [P, WS, 1024], F32R)
        wl, _ = own("wl", [P, WS, 1024], F32R)
        qT, qreg = own("qT", [P, NH, T])
        kT, kreg = own("kT", [P, NH, T])
        V, _ = own("V", [P, NT, NH * DV])
        con, _ = own("con", [P, N_CONST])
        par, _ = own("par", [P, N_PARAM])
        identb, _ = own("identb", [P, P], BF16)
        maskb, _ = own("maskb", [P, P], BF16)
        tabs, _ = own("tabs", [P, 4, NT, ROPE])
        acc, _ = own("acc", [P, T])
        sq0, sqreg = own("sq0", [P, T])
        tmp, tmpreg = own("tmp", [P, T])
        rstd, _ = own("rstd", [P, T])
        gate, _ = own("gate", [P, 2, T])
        raw, _ = own("raw", [P, 2, T])
        qn, _ = own("qn", [P, 3, HG * QK])
        rt, _ = own("rt", [P, 2, HG * ROPE])
        ust, _ = own("ust", [P, 20, HG])
        uss, _ = own("uss", [P, 3, HG])
        krg, _ = own("krg", [P, NT, ROPE])
        small, _ = own("small", [P, 72])
        assert at[0] <= nc.sbuf_usable_end, (at[0], nc.sbuf_usable_end)

        sq1 = over("sq1", [P, T], tmpreg)
        sqx = over("sqx", [P, T], sqreg)
        lo = yreg + KT * TB4
        ch, cl = over("ch", [P, 3, T], yreg, F32R), over("cl", [P, 3, T], lo, F32R)
        ckv = over("ckv", [P, T], yreg + 3 * TB4)
        cu = [over("cu0", [P, T], yreg + 3 * TB4), over("cu1", [P, T], lo + 4 * TB4 + NT * RH * RD * 4)]
        kr = over("kr", [P, NT, ROPE], lo + 5 * TB4 + NT * RH * RD * 4)
        cacc = [over("ca0", [P, T], lo + 2 * TB4), over("ca1", [P, T], lo + 3 * TB4)]
        rqk = over("rqk", [P, 4, T], yreg + 4 * TB4)
        vtok = over("vtok", [P, NT, RH * RD], lo + 4 * TB4)
        krT = over("krT", [P, T], kreg)
        hoff = [hreg]

        def over_h(name, shape):
            size = 4
            for s in shape[1:]:
                size *= s
            t = over(name, shape, hoff[0])
            hoff[0] += size + (-size) % 32
            assert hoff[0] <= hreg + 2 * KT * TB4
            return t

        SC_OFF = [0, 528, 928, 1200, 1344]
        sc = over_h("sc", [P, 2, 1360])
        ort = over_h("ort", [P, NT, RH * RD])
        pb = over_h("pb", [P, 3, T])
        pt = over_h("pt", [P, 3, 512])
        ptm = over_h("ptm", [P, 2, P])
        yo = over_h("yo", [P, NH * DV])
        nmax = over_h("nmax", [P, NT * NH])
        esum = over_h("esum", [P, NT * NH])
        tb = over("tb", [P, 2, T], qreg)
        ts = over("ts", [P, 2, T], qreg + 2 * TB4)
        xin = over("xin", [P, 4, D], qreg)
        xmeta = over("xmeta", [P, D], kreg)
        mneg = over("mneg", [P, P], kreg + 4 * D)
        xout = over("xout", [P, 4, D], qreg)

        ps = ctx.enter_context(nc.psum_tensor("ps", [P, 8, 512], F32))
        psf = ps[:, :, :].rearrange("p b c -> p (b c)")

        def C(name, rows=P):
            o, w = CONSTS[name]
            return con[0:rows, o:o + w]

        def PAR(name, i=0, rows=P):
            o, _ = PARAMS[name]
            return par[0:rows, o + i:o + i + 1]

        def pair(b):
            return ps[:, b:b + 2, 0:TH]

        def two(ap):
            return ap.rearrange("p (a b) -> p a b", a=2)

        def s_bank(item):
            return 4 + 2 * (item % 2)

        def item_no(u):
            return u if u < NH else u + 2

        def o_bank(tt):
            return 3 - tt % 2

        def meta_keys(u):
            if u < NH:
                return ps[0:META, 2, 0:META]
            return ps[0:META, s_bank(item_no(u)) + 1, META:META + P]

        ident = C("ident")
        lat_sq = [sq0, tmp, acc]
        btile = [sq0, tmp]

        con_in = sem("con_in")
        settled = sem("settled")
        x_in = sem("x_in")
        par_in = sem("par_in")
        stage_in = [sem(f"stage_in{i}") for i in range(SS)]
        setup = sem("setup")
        w_hi = sem("w_hi")
        w_lo = sem("w_lo")
        t_done = sem("t_done")
        t_read = sem("t_read")
        xt_done = sem("xt_done")
        xt_read = sem("xt_read")
        xa_new, xa_hi, xa_lo, xa_sq = sem("xa_new"), sem("xa_hi"), sem("xa_lo"), sem("xa_sq")
        xm_new, xm_hi, xm_lo, xm_sq = sem("xm_new"), sem("xm_hi"), sem("xm_lo"), sem("xm_sq")
        ms_done = sem("ms_done")
        std_new = sem("std_new")
        s_new, s_hi, s_lo = sem("s_new"), sem("s_hi"), sem("s_lo")
        tabs_new = sem("tabs_new")
        raw_new, raw_sq, raw_ms = sem("raw_new"), sem("raw_sq"), sem("raw_ms")
        lat_std, lat_new, lat_hi, lat_lo = sem("lat_std"), sem("lat_new"), sem("lat_hi"), sem("lat_lo")
        kr_tr, kr_read, kr_ss = sem("kr_tr"), sem("kr_read"), sem("kr_ss")
        u_done, u_sq, u_ss, u_std, u_read, u_tok = (sem("u_done"), sem("u_sq"), sem("u_ss"), sem("u_std"),
                                                    sem("u_read"), sem("u_tok"))
        tr_done, tr_read = sem("tr_done"), sem("tr_read")
        rq_new, rp_done, rp_read = sem("rq_new"), sem("rp_done"), sem("rp_read")
        rv_tr, rv_read = sem("rv_tr"), sem("rv_read")
        gz_new, gate_new = sem("gz_new"), sem("gate_new")
        yc_new, yc_hi, yc_lo = sem("yc_new"), sem("yc_hi"), sem("yc_lo")
        rs_done, rs_read, rs_mask, ro_done, ro_read, ro_ss, ro_std, ro_tok, ry_tr, yr_new, yr_hi, yr_lo = (
            sem(n) for n in ("rs_done", "rs_read", "rs_mask", "ro_done", "ro_read", "ro_ss", "ro_std", "ro_tok",
                             "ry_tr", "yr_new", "yr_hi", "yr_lo"))
        a_s, a_max, a_exp, a_tr, a_pt, a_ptm, a_pv, a_o, a_ytr, ya_hi, ya_lo = (
            sem(n) for n in ("a_s", "a_max", "a_exp", "a_tr", "a_pt", "a_ptm", "a_pv", "a_o", "a_ytr",
                             "ya_hi", "ya_lo"))
        fin_tr, fin_read, out_done = sem("fin_tr"), sem("fin_read"), sem("out_done")

        def settle(eng):
            eng.sem_inc(settled, 1)

        def tile_no(l, n):
            return (l + 1) * L_TILES + n + 1

        def half_no(l, i):
            return l * L_HALVES + i + 1

        W_PRIME = 2

        def grp(l, g, n, per=GT):
            return l * 0 + (l * NGRP + g) * per + n + 1

        block = ctx.enter_context(nc.Block())

        @block.sync
        def _(sp):
            sp.dma_start(con[:, :], consts).then_inc(con_in, 16)
            sp.dma_start(mneg[:, :], maskneg).then_inc(con_in, 16)
            sp.dma_start(par[:, :], params[0]).then_inc(par_in, 16)
            sp.dma_start(xmeta[0:META, :], meta).then_inc(x_in, 16)
            sp.dma_start(xin[:, :, :], x[0].rearrange("(t p) d -> p t d", p=P)).then_inc(x_in, 16)

            def load(l, j, dst, src):
                sp.wait_ge(w_lo, W_PRIME + l * L_HALVES + 2 * (j - 1))
                settle(sp)
                sp.dma_start(dst, src).then_inc(stage_in[j % SS], 16)

            def slab(j, w=256):
                return stage[:, j % SS, 0:KT * w].rearrange("p (k n) -> p k n", k=KT)

            with sp.Fori(0, DEPTH) as l:
                def win(col, w=256):
                    return w_in[l, :, col:col + w].rearrange("(k p) n -> p k n", p=P)

                def uq(c):
                    return w_uq[l, :, c * HG * QK:(c + 1) * HG * QK].rearrange("(k p) n -> p k n", p=P)

                load(l, 0, slab(0), win(OFF_CQ))
                load(l, 1, slab(1, 160), win(OFF_CKV, 160))
                load(l, 2, slab(2), win(OFF_RQ))
                load(l, 3, stage[:, 1, 0:2 * HG * QK].rearrange("p (k n) -> p k n", k=2), uq(0))
                load(l, 4, slab(4), win(OFF_RK))
                load(l, 5, slab(5), win(OFF_RV))
                load(l, 6, stage[:, 0, 0:2 * HG * QK].rearrange("p (k n) -> p k n", k=2), uq(1))
                load(l, 7, slab(7), win(OFF_RG))
                load(l, 8, stage[:, 0, 0:1024], w_ukv[l])
                for j, col in ((9, OFF_C), (10, OFF_H), (11, OFF_B)):
                    load(l, j, slab(j), win(col))
                for c in range(4):
                    load(l, 12 + c, slab(12 + c),
                         w_out[l, :, c * 256:(c + 1) * 256].rearrange("(k p) n -> p k n", p=P))

                def group(g):
                    for c in range(4):
                        sp.wait_ge(w_lo, W_PRIME + l * L_HALVES + PRE_HALVES + g * GT + 2 * (c - 1))
                        settle(sp)
                        sp.dma_start(slab(c), w_mlp_in[l, :, bass.ds(g * FG + c * 256, 256)]
                                     .rearrange("(k p) n -> p k n", p=P)).then_inc(stage_in[c % SS], 16)
                    for c in range(4):
                        sp.wait_ge(w_lo, W_PRIME + l * L_HALVES + PRE_HALVES + g * GT + 2 * (c + 3))
                        settle(sp)
                        sp.dma_start(slab(c), w_mlp_out[l, bass.ds(g * FG, FG), c * 256:(c + 1) * 256]
                                     .rearrange("(k p) n -> p k n", p=P)).then_inc(stage_in[c % SS], 16)

                group(0)
                sp.wait_ge(xm_lo, l * KT + KT)
                settle(sp)
                sp.dma_start(par[:, :], params[l + 1]).then_inc(par_in, 16)
                with sp.Fori(1, NGRP - 1) as g:
                    group(g)
                group(NGRP - 1)

            for t in range(4):
                sp.wait_ge(fin_read, 2 * t + 2)
                sp.dma_start(out[0, t * P:(t + 1) * P, :], xout[:, t, :]).then_inc(out_done, 16)
            sp.wait_ge(out_done, 16 * 4)

        @block.tensor
        def _(pe):
            mm = nc.tensor.matmul
            pe.sem_inc(t_done, L_TILES)
            pe.wait_ge(con_in, 32)
            pe.wait_ge(x_in, 32)
            for k in range(KT):
                b = 2 * (k % 2)
                if k >= 2:
                    pe.wait_ge(xt_read, k - 1)
                nc.tensor.transpose(ps[:, b + 1, 0:META], xmeta[0:META, k * P:(k + 1) * P], ident[0:META, 0:META])
                for t in range(4):
                    last = nc.tensor.transpose(ps[:, b, t * P:(t + 1) * P], xin[:, t, k * P:(k + 1) * P], ident)
                last.then_inc(xt_done, 1)

            def gemm(no, half, slot, rh, rl, ready, cols=P, rows=KT):
                b = 2 * (no % 2)
                first = True
                for k in range(rows):
                    if ready:
                        ready(k)
                    for w, r in ((wh, rh), (wh, rl), (wl, rh)):
                        for c in range(2):
                            last = mm(ps[:, b + c, 0:TH], w[:, slot, k * P:(k + 1) * P],
                                      r[:, k, c * TH:(c + 1) * TH],
                                      start=(k == 0 and w is wh and r is rh), stop=(k == rows - 1 and w is wl))
                return last

            def tile(l, n, rh, rl, ready=None):
                pe.wait_ge(w_lo, W_PRIME + half_no(l, TILE_HALF[n]))
                pe.wait_ge(t_read, tile_no(l, n - 2))
                gemm(n, TILE_HALF[n], SLOT[TILE_HALF[n]], rh, rl, ready).then_inc(t_done, 1)

            def mean_square(first_bank):
                for c in range(2):
                    last = mm(ps[:, first_bank + c, 0:TH], C("ones"), acc[:, c * TH:(c + 1) * TH],
                              start=True, stop=True)
                last.then_inc(ms_done, 1)

            def group(l, g, kind):
                for m in range(GT):
                    pe.wait_ge(w_lo, W_PRIME + l * L_HALVES + PRE_HALVES + g * GT + m + 1)
                    pe.wait_ge(t_read, (l + 1) * L_TILES + PRE_TILES + g * GT + m - 1)
                    if m < 8:
                        def ready(k):
                            if kind == "first" and m == 0:
                                pe.wait_ge(xm_lo, l * KT + k + 1)
                        gemm(m, None, m % WS, hh, hl, ready).then_inc(t_done, 1)
                        if kind == "first" and m == 0:
                            pe.wait_ge(xm_sq, l + 1)
                            mean_square(4)
                    else:
                        def ready(k):
                            if m == 8:
                                pe.wait_ge(s_lo, (l * NGRP + g) * 8 + k + 1)
                        gemm(m, None, m % WS, yh, yl, ready).then_inc(t_done, 1)

            with pe.Fori(0, DEPTH) as l:
                def aux_free(item):
                    prev = AUX_PREV[item]
                    if prev is not None:
                        kind, i = prev
                        pe.wait_ge(u_read if kind == "u" else tr_read, l * 20 + i + 1)

                def unit(u):
                    b = AUX_BANK[("u", u)]
                    aux_free(("u", u))
                    c, tt = u // NT % 2, u % NT
                    t0 = TA[tt][0]
                    if u < 10:
                        if u == 0:
                            pe.wait_ge(lat_lo, l * 3 + 2)
                        if tt == 0:
                            pe.wait_ge(w_lo, W_PRIME + half_no(l, MLA_HALF[2 * c + 1]))
                        for k in range(2):
                            s = SLOT[MLA_HALF[2 * c + k]]
                            for a, w in ((ch, wh), (cl, wh), (ch, wl)):
                                last = mm(ps[:, b, 0:HG * QK], a[:, k, t0:t0 + P], w[:, s, 0:HG * QK],
                                          start=(k == 0 and a is ch and w is wh), stop=(k == 1 and w is wl))
                    else:
                        if u == 10:
                            pe.wait_ge(lat_lo, l * 3 + 3)
                        if tt == 0:
                            pe.wait_ge(w_lo, W_PRIME + half_no(l, MLA_HALF[4 + c]))
                        s = SLOT[MLA_HALF[4 + c]]
                        for a, w in ((ch, wh), (cl, wh), (ch, wl)):
                            last = mm(ps[:, b, :], a[:, 2, t0:t0 + P], w[:, s, 0:512],
                                      start=(a is ch and w is wh), stop=(w is wl))
                    last.then_inc(u_done, 1)

                def unit_transpose(u):
                    b = AUX_BANK[("tr", u)]
                    aux_free(("tr", u))
                    R = TA[u % NT][1]
                    pe.wait_ge(u_tok, l * 20 + u + 1)
                    settle(pe)
                    for h in range(HG):
                        last = nc.tensor.transpose(ps[0:QK, b, h * P:h * P + R],
                                                   qn[0:R, u % 3, h * QK:(h + 1) * QK], ident[0:R, 0:R])
                    last.then_inc(tr_done, 1)

                def gap(n):
                    for kind, i in GAPS.get(n, []):
                        (unit if kind == "u" else unit_transpose)(i)

                def swap_halves(i):
                    b = 4 + 2 * (i % 2)
                    pe.wait_ge(rq_new, l * 4 + i + 1)
                    if i >= 2:
                        pe.wait_ge(rp_read, l * 4 + i - 1)
                    for c in range(2):
                        last = mm(ps[:, b + c, 0:TH], C("perm"), rqk[:, i, c * TH:(c + 1) * TH],
                                  start=True, stop=True)
                    last.then_inc(rp_done, 1)

                for n in range(N_IN):
                    def ready(k):
                        if n == 0:
                            pe.wait_ge(xa_lo, l * KT + k + 1)
                    tile(l, n, hh, hl, ready)
                    if n == 0:
                        pe.wait_ge(xa_sq, l + 1)
                        mean_square(4)
                    if n == 4:
                        for i, ks in ((0, (0, 1)), (1, (2,))):
                            b = 6 if i == 0 else 4
                            if i == 1:
                                pe.wait_ge(std_new, 2 * l + 1)
                            for k in ks:
                                pe.wait_ge(raw_sq, l * 3 + k + 1)
                                for c in range(2):
                                    last = mm(ps[:, b + c, 0:TH], C("ones"),
                                              lat_sq[k][:, c * TH:(c + 1) * TH],
                                              start=(k == ks[0]), stop=(k == ks[-1]))
                            last.then_inc(raw_ms, 1)
                    if n == 5:
                        pe.wait_ge(lat_std, l * 2 + 1)
                        pe.wait_ge(raw_new, l * 4 + 4)
                        settle(pe)
                        for tt, (t0, R) in enumerate(TA):
                            last = nc.tensor.transpose(ps[0:R, 6, tt * ROPE:(tt + 1) * ROPE],
                                                       krT[96:P, t0:t0 + R], ident[96:P, 96:P])
                        last.then_inc(kr_tr, 1)
                    if n == 6:
                        pe.wait_ge(lat_std, l * 2 + 2)
                        pe.wait_ge(kr_read, l + 1)
                    gap(n)
                    if n == 14:
                        pe.wait_ge(tr_read, l * 20 + 20)
                        swap_halves(0)
                        swap_halves(1)
                    if n == 15:
                        swap_halves(2)
                        swap_halves(3)
                    if n == 16:
                        pe.wait_ge(gz_new, l * 4 + 2)
                        pe.wait_ge(rp_read, l * 4 + 4)
                        for it, (t0, R) in enumerate(TB):
                            for f in range(2):
                                o = (it % 2) * 256 + f * P
                                last = nc.tensor.transpose(ps[0:R, 4 + it // 2, o:o + P],
                                                           raw[:, f, t0:t0 + R], ident)
                        last.then_inc(rv_tr, 1)

                def ret_scores(h):
                    f, r = h // 2, RD * (h % 2)
                    kk, qq = rqk[r:r + RD, 2 + f, :], rqk[r:r + RD, f, :]
                    if h == 0:
                        pe.wait_ge(rv_read, l + 1)
                        pe.wait_ge(rp_read, l * 4 + 4)
                    if h >= 1:
                        pe.wait_ge(rs_read, l * 16 + 4 * (h - 1) + 1)
                    for c in range(2):
                        last = mm(ps[:, 4 + c, 0:TH], kk[:, 0:P], qq[:, c * TH:(c + 1) * TH], start=True, stop=True)
                    last.then_inc(rs_done, 1)
                    if h >= 1:
                        pe.wait_ge(rs_read, l * 16 + 4 * (h - 1) + 2)
                    mm(ps[:, 6, 0:T - P], kk[:, P:2 * P], qq[:, P:T], start=True, stop=True).then_inc(rs_done, 1)
                    if h >= 1:
                        pe.wait_ge(rs_read, l * 16 + 4 * (h - 1) + 4)
                    o = 0
                    for j in (2, 3, 4):
                        j0, R = TB[j]
                        last = mm(ps[0:R, 7, o:o + T - j0], kk[:, j0:j0 + R], qq[:, j0:T], start=True, stop=True)
                        o += T - j0
                    last.then_inc(rs_done, 1)

                def ret_sum(h):
                    pe.wait_ge(rs_mask, l * 4 + h + 1)
                    if h == 0:
                        pe.wait_ge(t_read, tile_no(l, N_IN - 1))
                    for it, (i0, R) in enumerate(TB):
                        for jt in range(it + 1):
                            j0, K = TB[jt]
                            o = SC_OFF[jt] + i0 - j0
                            b, o2 = 2 * (h // 2) + it // 4, (it % 4) * P + (h % 2) * RD
                            last = mm(ps[0:R, b, o2:o2 + RD],
                                      sc[0:K, h % 2, o:o + R], vtok[0:K, jt, h * RD:(h + 1) * RD],
                                      start=(jt == 0), stop=(jt == it))
                    last.then_inc(ro_done, 1)

                ret_scores(0)
                ret_scores(1)
                ret_sum(0)
                ret_scores(2)
                ret_sum(1)
                ret_scores(3)
                ret_sum(2)
                ret_sum(3)

                def scores(u):
                    tt, h = u // NH, u % NH
                    q0, R = TA[tt]
                    L = q0 + R
                    it = item_no(u)
                    b = s_bank(it)
                    if it < 2:
                        pe.wait_ge(rs_read, l * 16 + 16)
                    elif it in (10, 11):
                        pe.wait_ge(yr_new, l * 2 + it - 9)
                    else:
                        pe.wait_ge(a_exp, l * 40 + (it - 2 if it < 10 else it - 4) + 1)
                    if u == 0:
                        pe.wait_ge(tr_read, l * 20 + 20)
                    n0 = min(L, 512)
                    q = qT[0:QK, h, q0:q0 + R]
                    pieces = [(0, n0)] + ([(512, L)] if L > 512 else [])
                    d0 = q0 if tt else 0
                    for i, (c0, c1) in enumerate(pieces):
                        if i:
                            pe.wait_ge(a_ptm, l * 40 + u - 1)
                        mm(psf[0:R, b * 512 + c0:b * 512 + c1], q, kT[0:QK, h, c0:c1], start=True, stop=False)
                        m0 = max(c0, d0)
                        last = mm(psf[0:R, b * 512 + m0:b * 512 + c1], identb[0:R, 0:R],
                                  maskb[0:R, m0 - d0:c1 - d0], start=False, stop=True)
                    last.then_inc(a_s, 1)

                def p_transpose(u):
                    tt, h = u // NH, u % NH
                    R = TA[tt][1]
                    pe.wait_ge(a_exp, l * 40 + u + 1)
                    if u == 0:
                        pe.wait_ge(ro_read, l * 4 + 4)
                    if tt:
                        if u >= 10:
                            pe.wait_ge(a_pt, l * 32 + u - 10 + 1)
                        for b in range(1, tt + 1):
                            nc.tensor.transpose(ps[:, u % 2, (b - 1) * P:b * P],
                                                pb[:, u % 3, META + (b - 1) * P:META + b * P], ident)
                    if u >= 1:
                        pe.wait_ge(a_ptm, l * 40 + (u if u < NH else u - 1))
                    settle(pe)
                    nc.tensor.transpose(meta_keys(u), pb[0:R, u % 3, 0:META],
                                        ident[0:R, 0:R]).then_inc(a_tr, 1)

                def p_v(u):
                    tt, h = u // NH, u % NH
                    R = TA[tt][1]
                    pe.wait_ge(a_ptm, l * 40 + u + 1)
                    if tt:
                        pe.wait_ge(a_pt, l * 32 + u - 8 + 1)
                    if h == 0 and tt >= 2:
                        pe.wait_ge(ya_lo, l * NT + tt - 1)
                    settle(pe)
                    o = ps[0:R, o_bank(tt), h * DV:(h + 1) * DV]
                    last = mm(o, ptm[0:META, u % 2, 0:R], V[0:META, 0, h * DV:(h + 1) * DV],
                              start=True, stop=(tt == 0))
                    for b in range(1, tt + 1):
                        last = mm(o, pt[:, u % 3, (b - 1) * P:b * P], V[:, b, h * DV:(h + 1) * DV],
                                  start=False, stop=(b == tt))
                    last.then_inc(a_pv, 1)

                def y_transpose(tt):
                    R = TA[tt][1]
                    pe.wait_ge(a_o, l * NT + tt + 1)
                    settle(pe)
                    for f in range(4):
                        last = nc.tensor.transpose(ps[:, o_bank(tt), f * P:f * P + R], yo[0:R, f * P:(f + 1) * P],
                                                   ident[0:R, 0:R])
                    last.then_inc(a_ytr, 1)

                scores(0)
                scores(1)
                for u in range(40):
                    p_transpose(u)
                    if u == 6:
                        for f in range(2):
                            pe.wait_ge(ro_tok, l + 1)
                            pe.wait_ge(a_exp, l * 40 + 7 + f)
                            for it, (t0, R) in enumerate(TB):
                                last = nc.tensor.transpose(psf[:, (4 + 2 * f) * 512 + t0:(4 + 2 * f) * 512 + t0 + R],
                                                           ort[0:R, it, f * P:(f + 1) * P], ident[0:R, 0:R])
                            last.then_inc(ry_tr, 1)
                    if u + 2 < 40 and u not in (6, 7):
                        scores(u + 2)
                    if u == 7:
                        scores(8)
                        scores(9)
                    if u >= 1:
                        p_v(u - 1)
                    if u % NH == 3 and u > NH:
                        y_transpose(u // NH - 1)
                p_v(39)
                y_transpose(NT - 1)

                for n in range(N_IN, PRE_TILES):
                    def ready(k):
                        if n == N_IN:
                            if k < 2:
                                pe.wait_ge(yc_lo, l * 2 + k + 1)
                            elif k < 4:
                                pe.wait_ge(yr_lo, l * 2 + k - 1)
                            elif k == 4:
                                pe.wait_ge(ya_lo, l * NT + NT)
                    tile(l, n, yh, yl, ready)

                group(l, 0, "first")
                with pe.Fori(1, NGRP - 1) as g:
                    group(l, g, "middle")
                group(l, NGRP - 1, "last")

            pe.wait_ge(xa_new, (DEPTH + 1) * KT)
            pe.wait_ge(t_read, (DEPTH + 1) * L_TILES)
            for t in range(4):
                for f in range(2):
                    i = 2 * t + f
                    if i >= 4:
                        pe.wait_ge(fin_read, i - 3)
                    for k in range(4):
                        last = nc.tensor.transpose(ps[:, i % 4, k * P:(k + 1) * P],
                                                   xT[:, 4 * f + k, META + t * P:META + (t + 1) * P], ident)
                    last.then_inc(fin_tr, 1)

        def pt_read(eng, copy, l, u):
            tt = u // NH
            eng.wait_ge(a_tr, l * 40 + u + 1)
            if u - 3 >= NH:
                eng.wait_ge(a_pv, l * 40 + u - 2)
            src, dst = ps[:, u % 2, 0:tt * P], pt[:, u % 3, 0:tt * P]
            if u > NH:
                eng.wait_ge(a_pt, l * 32 + u - 8)
            if copy is None:
                nc.vector.tensor_copy(dst, src).then_inc(a_pt, 1)
            else:
                copy(dst, src, ACT.Copy).then_inc(a_pt, 1)

        def y_hi(act, A, l, tt):
            t0, R = TA[tt]
            act.wait_ge(a_ytr, l * NT + tt + 1)
            A(yh[:, 4:8, t0:t0 + R], ps[:, o_bank(tt), :].rearrange("p (f t) -> p f t", f=4)[:, :, 0:R],
              ACT.Copy).then_inc(ya_hi, 1)

        @block.scalar
        def _(act):
            A = nc.scalar.activation
            act.wait_ge(con_in, 32)
            act.wait_ge(par_in, 16)

            def x_split(g, k, sem_new, sem_hi, value):
                act.wait_ge(sem_new, value)
                A(hh[:, k, :], xT[:, k, :], ACT.Copy, scale=PAR(g, k)).then_inc(sem_hi, 1)

            for k in range(KT):
                x_split("attn_g", k, xa_new, xa_hi, k + 1)

            def source(i):
                st = stage[:, (i // 2) % SS, :]
                h = i % 2
                if HALVES[i] == ("T", 2):
                    return st[:, 0:KT * 160].rearrange("p (k n) -> p k n", k=KT)[:, :, 0:P], KT
                if HALVES[i] == ("T", 3):
                    return st[:, 0:KT * 160].rearrange("p (k n) -> p k n", k=KT)[:, :, 32:160], KT
                if HALVES[i][0] == "T":
                    return st.rearrange("p (k n) -> p k n", k=KT)[:, :, h * P:(h + 1) * P], KT
                w = HG * QK if HALVES[i][1] < 4 else 512
                return st[:, h * w:(h + 1) * w], w

            def hi(l, i):
                src, n = source(i)
                dst = wh[:, SLOT[i], :].rearrange("p (k n) -> p k n", k=KT) if n == KT else wh[:, SLOT[i], 0:n]
                j = i // 2
                act.wait_ge(stage_in[j % SS], 16 * (l * (L_BLOCKS // 2) + j // 2 + 1))
                if i < 4:
                    act.wait_ge(t_done, tile_no(l, i - 4))
                else:
                    kind, n = FREED[i]
                    if kind == "T":
                        act.wait_ge(t_done, tile_no(l, n))
                    else:
                        act.wait_ge(u_done, l * 20 + n + 1)
                A(dst, src, ACT.Copy).then_inc(w_hi, 1)

            def mlp_hi(l, g, m, freed):
                j = m // 2
                act.wait_ge(stage_in[j % SS], 16 * (l * (L_BLOCKS // 2) + PRE_BLOCKS // 2 + g * 4 + j // 2 + 1))
                act.wait_ge(t_done, freed)
                A(wh[:, m % WS, :].rearrange("p (k n) -> p k n", k=KT),
                  stage[:, j % SS, :].rearrange("p (k n) -> p k n", k=KT)[:, :, (m % 2) * P:(m % 2 + 1) * P],
                  ACT.Copy).then_inc(w_hi, 1)

            def root(value):
                act.wait_ge(ms_done, value)
                A(two(tmp[:, :]), pair(4), ACT.Sqrt, bias=C("eps"), scale=1.0 / D).then_inc(std_new, 1)

            def group(l, g, kind):
                for m in range(GT):
                    if kind != "last" or m < GT - 4:
                        mlp_hi(l, g if m < GT - 4 else g + 1, (m + 4) % GT,
                               (l + 1) * L_TILES + PRE_TILES + g * GT + m + 1)
                    if kind == "first" and m == 0:
                        root(2 * l + 2)
                    if m < 8:
                        act.wait_ge(s_new, (l * NGRP + g) * 8 + m + 1)
                        A(yh[:, m, :], ts[:, m % 2, :], ACT.Copy).then_inc(s_hi, 1)
                    elif kind == "last":
                        if m == 8:
                            act.wait_ge(par_in, 16 * (l + 2))
                        x_split("attn_g", m - 8, xa_new, xa_hi, (l + 1) * KT + m - 7)

            with act.Fori(0, DEPTH) as l:
                def unit(u):
                    b = AUX_BANK[("u", u)]
                    c, tt = u // NT % 2, u % NT
                    R = TA[tt][1]
                    s = [sq0, sq1][u % 2]
                    if u == 0:
                        act.wait_ge(kr_ss, l + 1)
                    act.wait_ge(u_done, l * 20 + u + 1)
                    if u >= 10:
                        A(V[0:R, tt, c * HG * DV:(c + 1) * HG * DV].rearrange("p (h d) -> p h d", h=HG),
                          ps[0:R, b, :].rearrange("p (h d) -> p h d", h=HG)[:, :, NOPE:], ACT.Copy)
                    if u >= 2:
                        act.wait_ge(u_ss, l * 20 + u - 1)
                    if u < 10:
                        A(s[0:R, 0:HG * QK], ps[0:R, b, 0:HG * QK], ACT.Square).then_inc(u_sq, 1)
                    else:
                        A(s[0:R, 0:HG * NOPE].rearrange("p (h d) -> p h d", h=HG),
                          ps[0:R, b, :].rearrange("p (h d) -> p h d", h=HG)[:, :, 0:NOPE],
                          ACT.Square).then_inc(u_sq, 1)

                def unit_root(u):
                    tt = u % NT
                    R = TA[tt][1]
                    act.wait_ge(u_ss, l * 20 + u + 1)
                    if u < 10:
                        A(ust[0:R, u, :], uss[0:R, u % 3, :], ACT.Sqrt, bias=C("eps_q", R),
                          scale=1.0).then_inc(u_std, 1)
                    else:
                        A(ust[0:R, u, :], uss[0:R, u % 3, :], ACT.Sqrt, bias=small[0:R, 8 + tt:9 + tt],
                          scale=1.0 / QK).then_inc(u_std, 1)

                def unit_read(u):
                    b = AUX_BANK[("tr", u)]
                    c, tt = u // NT % 2, u % NT
                    t0, R = TA[tt]
                    act.wait_ge(tr_done, l * 20 + u + 1)
                    dst, g = (qT, "qh_g") if u < 10 else (kT, "kh_g")
                    A(dst[0:QK, c * HG:(c + 1) * HG, t0:t0 + R],
                      ps[0:QK, b, :].rearrange("p (h t) -> p h t", h=HG)[:, :, 0:R], ACT.Copy,
                      scale=PAR(g, 0, QK)).then_inc(tr_read, 1)

                def conv_hi(f):
                    act.wait_ge(yc_new, l * 2 + f + 1)
                    A(yh[:, f, :], btile[f][:, :], ACT.Copy).then_inc(yc_hi, 1)

                for i in range(4):
                    hi(l, i)
                for n in range(N_IN - 1):
                    if n == 0:
                        root(2 * l + 1)
                    if n <= 2:
                        src = raw[:, n, :] if n < 2 else ckv[:, :]
                        act.wait_ge(raw_new, l * 4 + n + 1)
                        if n == 1:
                            act.wait_ge(tabs_new, l + 1)
                        A(lat_sq[n][:, :], src, ACT.Square).then_inc(raw_sq, 1)
                    if n == 4:
                        for i in LOADS[n]:
                            hi(l, i)
                        for i, (b, s, d) in enumerate(((6, Q_LORA, tmp), (4, KV_LORA, sq0))):
                            act.wait_ge(raw_ms, l * 2 + 2)
                            A(two(d[:, :]), pair(b), ACT.Sqrt, bias=C("eps"), scale=1.0 / s).then_inc(lat_std, 1)
                        for k in range(3):
                            act.wait_ge(lat_new, l * 3 + k + 1)
                            A(ch[:, k, :], [raw[:, 0, :], raw[:, 1, :], ckv[:, :]][k], ACT.Copy).then_inc(lat_hi, 1)
                    items = GAPS.get(n, [])
                    for kind, i in items:
                        if kind == "tr":
                            unit_read(i)
                    us = [i for kind, i in items if kind == "u"]
                    for i in us[:2]:
                        unit(i)
                    for j, i in enumerate(us):
                        unit_root(i)
                        if j == 0 and len(us) == 3:
                            unit(us[2])
                    if n == 16:
                        conv_hi(0)
                    if n == 15:
                        for f in range(2):
                            act.wait_ge(gz_new, l * 4 + 3 + f)
                            A(gate[:, f, :], gate[:, f, :], ACT.Silu).then_inc(gate_new, 1)
                    if n != 4:
                        for i in LOADS[n]:
                            hi(l, i)

                for h in range(RH):
                    if h >= 2:
                        act.wait_ge(ro_done, l * 4 + h - 1)
                    act.wait_ge(rs_done, l * 12 + 3 * h + 1)
                    A(two(sc[:, h % 2, 0:T]), pair(4), ACT.Copy).then_inc(rs_read, 1)
                    act.wait_ge(rs_done, l * 12 + 3 * h + 2)
                    A(sc[:, h % 2, T:T + 400], ps[:, 6, 0:400], ACT.Copy).then_inc(rs_read, 1)
                    act.wait_ge(rs_done, l * 12 + 3 * h + 3)
                    A(sc[:, h % 2, 928:928 + 416], ps[:, 7, 0:416], ACT.Copy).then_inc(rs_read, 1)
                    A(sc[0:META, h % 2, 1344:1360], ps[0:META, 7, 416:432], ACT.Copy).then_inc(rs_read, 1)
                    if h == 0:
                        conv_hi(1)
                        for i in LOADS[N_IN - 1]:
                            hi(l, i)

                act.wait_ge(ro_ss, l + 1)
                A(small[:, 32:52], small[:, 52:72], ACT.Sqrt, bias=C("eps"), scale=1.0 / RD).then_inc(ro_std, 1)

                for u in range(40):
                    tt, h = u // NH, u % NH
                    q0, R = TA[tt]
                    L = q0 + R
                    it = u if u < NH else u + 2
                    b = 4 + 2 * (it % 2)
                    act.wait_ge(a_max, l * 40 + u + 1)
                    if u >= 3:
                        act.wait_ge(a_tr, l * 40 + u - 2)
                    A(pb[0:R, u % 3, 0:L], psf[0:R, b * 512:b * 512 + L], ACT.Exp,
                      bias=nmax[0:R, u:u + 1], accum_out=esum[0:R, u:u + 1]).then_inc(a_exp, 1)
                    if u - 1 >= NH and (u - 1) % 2 == 1:
                        pt_read(act, A, l, u - 1)
                    if u == 9:
                        for f in range(2):
                            act.wait_ge(yr_new, l * 2 + f + 1)
                            A(yh[:, 2 + f, :], gate[:, f, :], ACT.Copy).then_inc(yr_hi, 1)
                    if h == 5 and tt:
                        y_hi(act, A, l, tt - 1)
                pt_read(act, A, l, 39)
                y_hi(act, A, l, NT - 1)

                for n in range(N_IN, PRE_TILES):
                    x_split("mlp_g", n - N_IN, xm_new, xm_hi, l * KT + n - N_IN + 1)
                    if n in LOADS:
                        for i in LOADS[n]:
                            hi(l, i)
                    else:
                        mlp_hi(l, 0, n - 22, tile_no(l, n))

                group(l, 0, "first")
                with act.Fori(1, NGRP - 1) as g:
                    group(l, g, "middle")
                group(l, NGRP - 1, "last")

            for i in range(1, 8, 2):
                act.wait_ge(fin_tr, i + 1)
                t, f = i // 2, i % 2
                act.wait_ge(fin_read, i)
                A(xout[:, t, f * 512:(f + 1) * 512], ps[:, i % 4, :], ACT.Copy).then_inc(fin_read, 1)

        @block.vector
        def _(dve):
            TT = nc.vector.tensor_tensor
            TS = nc.vector.tensor_scalar
            STT = nc.vector.scalar_tensor_tensor
            copy = nc.vector.tensor_copy
            drain = nc.vector.drain
            dve.sem_inc(t_read, L_TILES)
            dve.sem_inc(w_lo, W_PRIME)
            dve.wait_ge(con_in, 32)
            dve.wait_ge(par_in, 16)
            copy(identb[:, :], ident)
            copy(maskb[:, :], mneg[:, :])
            nc.vector.memset(small[:, :], 1.0)

            def x_low(g, k, sem_hi, sem_lo, value):
                dve.wait_ge(sem_hi, value)
                STT(hl[:, k, :], xT[:, k, :], PAR(g, k), hh[:, k, :].bitcast(F32), ALU.mult,
                    ALU.subtract).then_inc(sem_lo, 1)

            for k in range(KT):
                b = 2 * (k % 2)
                dve.wait_ge(xt_done, k + 1)
                copy(xT[:, k, 0:META], ps[:, b + 1, 0:META])
                copy(xT[:, k, META:T], ps[:, b, :]).then_inc(xt_read, 1)
                drain()
                dve.sem_inc(xa_new, 1)
                if k:
                    x_low("attn_g", k - 1, xa_hi, xa_lo, k)
            x_low("attn_g", KT - 1, xa_hi, xa_lo, KT)

            def source(i):
                st = stage[:, (i // 2) % SS, :]
                h = i % 2
                if HALVES[i] == ("T", 2):
                    return st[:, 0:KT * 160].rearrange("p (k n) -> p k n", k=KT)[:, :, 0:P], KT
                if HALVES[i] == ("T", 3):
                    return st[:, 0:KT * 160].rearrange("p (k n) -> p k n", k=KT)[:, :, 32:160], KT
                if HALVES[i][0] == "T":
                    return st.rearrange("p (k n) -> p k n", k=KT)[:, :, h * P:(h + 1) * P], KT
                w = HG * QK if HALVES[i][1] < 4 else 512
                return st[:, h * w:(h + 1) * w], w

            def low(l, i):
                dve.wait_ge(w_hi, half_no(l, i))
                src, n = source(i)
                s = SLOT[i]
                if n == KT:
                    h, o = (w[:, s, :].rearrange("p (k n) -> p k n", k=KT) for w in (wh, wl))
                else:
                    h, o = (w[:, s, 0:n] for w in (wh, wl))
                TT(o, src, h.bitcast(F32), ALU.subtract).then_inc(w_lo, 1)

            def mlp_low(l, g, m):
                dve.wait_ge(w_hi, l * L_HALVES + PRE_HALVES + g * GT + m + 1)
                h, o = (w[:, m % WS, :].rearrange("p (k n) -> p k n", k=KT) for w in (wh, wl))
                src = stage[:, (m // 2) % SS, :].rearrange("p (k n) -> p k n", k=KT)
                TT(o, src[:, :, (m % 2) * P:(m % 2 + 1) * P], h.bitcast(F32), ALU.subtract).then_inc(w_lo, 1)

            def invert(value):
                dve.wait_ge(std_new, value)
                nc.vector.reciprocal(rstd[:, :], tmp[:, :])
                drain()

            def x_add(k, no, value, done):
                dve.wait_ge(t_done, value)
                TT(two(xT[:, k, :]), pair(2 * (no % 2)), two(xT[:, k, :]), ALU.add).then_inc(t_read, 1)
                drain()
                if done is not None:
                    dve.sem_inc(done, 1)

            def group(l, g, kind):
                for m in range(GT):
                    value = (l + 1) * L_TILES + PRE_TILES + g * GT + m + 1
                    if m < 8:
                        if kind == "first" and m == 0:
                            invert(2 * l + 2)
                        dve.wait_ge(t_done, value)
                        TT(two(tb[:, m % 2, :]), pair(2 * (m % 2)), two(rstd[:, :]), ALU.mult).then_inc(t_read, 1)
                        drain()
                        STT(ts[:, m % 2, :], tb[:, m % 2, :], 0.0, tb[:, m % 2, :], ALU.max,
                            ALU.mult).then_inc(s_new, 1)
                    else:
                        x_add(m - 8, m, value, xa_new if kind == "last" else None)
                    if kind != "last" or m < GT - 4:
                        mlp_low(l, g if m < GT - 4 else g + 1, (m + 4) % GT)
                    if m < 8:
                        dve.wait_ge(s_hi, (l * NGRP + g) * 8 + m + 1)
                        TT(yl[:, m, :], ts[:, m % 2, :], yh[:, m, :].bitcast(F32), ALU.subtract).then_inc(s_lo, 1)
                    elif kind == "last":
                        if m == 8:
                            dve.wait_ge(par_in, 16 * (l + 2))
                        x_low("attn_g", m - 8, xa_hi, xa_lo, (l + 1) * KT + m - 7)

            with dve.Fori(0, DEPTH) as l:
                def unit_sum(u):
                    R = TA[u % NT][1]
                    w = QK if u < 10 else NOPE
                    dve.wait_ge(u_sq, l * 20 + u + 1)
                    if u >= 3:
                        dve.wait_ge(u_std, l * 20 + u - 2)
                    nc.vector.tensor_reduce(
                        uss[0:R, u % 3, :], [sq0, sq1][u % 2][0:R, 0:HG * w].rearrange("p (h d) -> p h d", h=HG),
                        AX, ALU.add).then_inc(u_ss, 1)

                def unit_norm(u):
                    b = AUX_BANK[("u", u)]
                    tt = u % NT
                    R = TA[tt][1]
                    dve.wait_ge(u_std, l * 20 + u + 1)
                    nc.vector.reciprocal(ust[0:R, u, :], ust[0:R, u, :])
                    drain()
                    if u >= 3:
                        dve.wait_ge(tr_done, l * 20 + u - 2)
                    o = qn[0:R, u % 3, :].rearrange("p (h d) -> p h d", h=HG)
                    r = ust[0:R, u, :].unsqueeze(2)
                    if u < 10:
                        TT(o, ps[0:R, b, 0:HG * QK].rearrange("p (h d) -> p h d", h=HG),
                           r.broadcast_to([R, HG, QK]), ALU.mult).then_inc(u_read, 1)
                        drain()
                        HR = ROPE // 2
                        tc, tsn = (rt[0:R, i, :].rearrange("p (h d) -> p h d", h=HG) for i in range(2))

                        def tab(i, a, c):
                            return tabs[0:R, i, tt, a:c].unsqueeze(1).broadcast_to([R, HG, c - a])

                        TT(tc, o[:, :, NOPE:QK], tab(0, 0, ROPE), ALU.mult)
                        TT(tsn[:, :, 0:HR], o[:, :, NOPE + HR:QK], tab(1, 0, HR), ALU.mult)
                        TT(tsn[:, :, HR:ROPE], o[:, :, NOPE:NOPE + HR], tab(1, HR, ROPE), ALU.mult)
                        drain()
                        TT(o[:, :, NOPE:QK], tc, tsn, ALU.add).then_inc(u_tok, 1)
                    else:
                        TT(o[:, :, 0:NOPE], ps[0:R, b, :].rearrange("p (h d) -> p h d", h=HG)[:, :, 0:NOPE],
                           r.broadcast_to([R, HG, NOPE]), ALU.mult).then_inc(u_read, 1)
                        TT(o[:, :, NOPE:QK], krg[0:R, tt, :].unsqueeze(1).broadcast_to([R, HG, ROPE]),
                           r.broadcast_to([R, HG, ROPE]), ALU.mult)
                        drain()
                        dve.sem_inc(u_tok, 1)

                def scaled(n, dst, rows=slice(0, P)):
                    dve.wait_ge(t_done, tile_no(l, n))
                    b = 2 * (n % 2)
                    return TT(two(dst), ps[rows, b:b + 2, 0:TH], two(rstd[rows, :]), ALU.mult)

                def rope(i):
                    dve.wait_ge(rp_done, l * 4 + i + 1)
                    TT(two(tmp[:, :]), pair(4 + 2 * (i % 2)), two(C("rope_s")), ALU.mult)
                    TT(rqk[:, i, :], rqk[:, i, :], C("rope_c"), ALU.mult)
                    drain()
                    TT(rqk[:, i, :], rqk[:, i, :], tmp[:, :], ALU.add)
                    drain()
                    dve.sem_inc(rp_read, 1)

                def conv_out(f):
                    TT(btile[f][:, :], btile[f][:, :], cacc[f][:, :], ALU.mult).then_inc(yc_new, 1)

                def conv_low(f):
                    dve.wait_ge(yc_hi, l * 2 + f + 1)
                    TT(yl[:, f, :], btile[f][:, :], yh[:, f, :].bitcast(F32), ALU.subtract).then_inc(yc_lo, 1)

                def freed():
                    drain()
                    dve.sem_inc(t_read, 1)

                def rope_tables():
                    for i, (g, t) in enumerate((("qrope_g", "tok_c"), ("qrope_g", "tok_s"), ("krope_g", "tok_c"),
                                                ("krope_g", "tok_s"))):
                        o = PARAMS[g][0]
                        t3 = C(t).rearrange("p (t d) -> p t d", t=NT)
                        if i % 2 == 0:
                            TT(tabs[:, i, :, :], t3, par[:, o:o + ROPE].unsqueeze(1).broadcast_to([P, NT, ROPE]),
                               ALU.mult)
                        else:
                            HR = ROPE // 2
                            for a, c in ((0, HR), (HR, 0)):
                                TT(tabs[:, i, :, a:a + HR], t3[:, :, a:a + HR],
                                   par[:, o + c:o + c + HR].unsqueeze(1).broadcast_to([P, NT, HR]), ALU.mult)

                for i in range(4):
                    low(l, i)
                rope_tables()
                invert(2 * l + 1)
                dve.sem_inc(tabs_new, 1)
                for n in range(N_IN - 1):
                    if n < 2:
                        scaled(n, raw[:, n, :])
                    elif n == 2:
                        scaled(n, ckv[:, :])
                    elif n == 3:
                        scaled(n, krT[96:P, :], slice(96, P))
                    elif n < 8:
                        scaled(n, rqk[:, n - 4, :])
                    elif n < 10:
                        scaled(n, raw[:, n - 8, :])
                    elif n < 12:
                        scaled(n, gate[:, n - 10, :])
                    elif n < 14:
                        scaled(n, cu[n - 12][:, :])
                    elif n < 16:
                        scaled(n, sq0[:, :])
                    else:
                        scaled(n, btile[0][:, :])
                    freed()
                    if n < 4:
                        dve.sem_inc(raw_new, 1)
                    if 4 <= n < 8:
                        dve.sem_inc(rq_new, 1)
                    if 8 <= n < 12:
                        dve.sem_inc(gz_new, 1)
                    if n == 15:
                        rope(2)
                        rope(3)
                    if n in (14, 15):
                        f = n - 14
                        TT(cu[f][:, :], cu[f][:, :], sq0[:, :], ALU.mult)
                        drain()
                        TS(cacc[f][:, :], cu[f][:, :], PAR("conv", 3 * f + 2), None, ALU.mult)
                        drain()
                        STT(cacc[f][:, 1:T], cu[f][:, 0:T - 1], PAR("conv", 3 * f + 1), cacc[f][:, 1:T],
                            ALU.mult, ALU.add)
                        drain()
                        STT(cacc[f][:, 2:T], cu[f][:, 0:T - 2], PAR("conv", 3 * f), cacc[f][:, 2:T],
                            ALU.mult, ALU.add)
                    if n == 4:
                        for i in LOADS[n]:
                            low(l, i)
                        for i, (s, d, ks) in enumerate(((tmp, acc, (0, 1)), (sq0, tmp, (2,)))):
                            dve.wait_ge(lat_std, l * 2 + 1 + i)
                            nc.vector.reciprocal(d[:, :], s[:, :])
                            drain()
                            for k in ks:
                                src = [raw[:, 0, :], raw[:, 1, :], ckv[:, :]][k]
                                g = PAR("qn_g", k) if k < 2 else PAR("kvn_g")
                                STT(src, src, g, d[:, :], ALU.mult, ALU.mult).then_inc(lat_new, 1)
                        for k in range(3):
                            dve.wait_ge(lat_hi, l * 3 + k + 1)
                            TT(cl[:, k, :], [raw[:, 0, :], raw[:, 1, :], ckv[:, :]][k], ch[:, k, :].bitcast(F32),
                               ALU.subtract).then_inc(lat_lo, 1)
                    if n == 5:
                        nc.vector.memset(kr[:, 0, :], 0.0)
                        drain()
                        dve.wait_ge(kr_tr, l + 1)
                        copy(kr[0:META, 0, :], ps[0:META, 6, 0:ROPE])
                        copy(kr[:, 1:NT, :], ps[:, 6, ROPE:NT * ROPE].rearrange("p (t d) -> p t d", d=ROPE))
                        drain()
                        dve.sem_inc(kr_read, 1)
                        HR = ROPE // 2
                        t1 = sq0[:, 0:NT * ROPE].rearrange("p (t d) -> p t d", t=NT)
                        t2 = tmp[:, 0:NT * ROPE].rearrange("p (t d) -> p t d", t=NT)
                        TT(t2, kr[:, :, :], kr[:, :, :], ALU.mult)
                        TT(krg[:, :, :], kr[:, :, :], tabs[:, 2, :, :], ALU.mult)
                        TT(t1[:, :, 0:HR], kr[:, :, HR:ROPE], tabs[:, 3, :, 0:HR], ALU.mult)
                        TT(t1[:, :, HR:ROPE], kr[:, :, 0:HR], tabs[:, 3, :, HR:ROPE], ALU.mult)
                        drain()
                        TT(krg[:, :, :], krg[:, :, :], t1, ALU.add)
                        nc.vector.tensor_reduce(small[:, 8:8 + NT], t2, AX, ALU.add)
                        drain()
                        TS(small[:, 8:8 + NT], small[:, 8:8 + NT], 1.0 / QK, EPS, ALU.mult, ALU.add)
                        drain()
                        dve.sem_inc(kr_ss, 1)
                    us = [i for kind, i in GAPS.get(n, []) if kind == "u"]
                    for i in us:
                        unit_sum(i)
                    for i in us:
                        unit_norm(i)
                    if n == 14:
                        rope(0)
                        rope(1)
                    if n == 16:
                        dve.wait_ge(rv_tr, l + 1)
                        for it, (t0, R) in enumerate(TB):
                            o = (it % 2) * 256
                            gi = CONSTS["g_in"][0] + it * RH
                            TT(vtok[0:R, it, :].rearrange("p (h d) -> p h d", h=RH),
                               ps[0:R, 4 + it // 2, o:o + 256].rearrange("p (h d) -> p h d", h=RH),
                               con[0:R, gi:gi + RH].unsqueeze(2).broadcast_to([R, RH, RD]), ALU.mult)
                        drain()
                        dve.sem_inc(rv_read, 1)
                    if n == 16:
                        conv_out(0)
                    if n != 4:
                        for i in LOADS[n]:
                            low(l, i)
                    if n == 16:
                        conv_low(0)

                def heads(ap, r, a, b, pair_no):
                    return ap[0:r, a:b, :].rearrange("p t (h d) -> p t h d", h=RH)[:, :, 2 * pair_no:2 * pair_no + 2, :]

                rsq = pt
                parts = ((P, 0, NT - 1), (TB[-1][1], NT - 1, NT))

                def ret_out(c):
                    dve.wait_ge(ro_done, l * 4 + 2 * c + 2)
                    o = CONSTS["g_out"][0]
                    decay = con[:, o:o + NT * RH].rearrange("p (t h) -> p t h", t=NT)
                    for i, (r, a, b) in enumerate(parts):
                        TT(heads(ort, r, a, b, c),
                           ps[0:r, 2 * c + i, 0:(b - a) * P].rearrange("p (t h d) -> p t h d", h=2, d=RD),
                           decay[0:r, a:b, 2 * c:2 * c + 2].unsqueeze(3).broadcast_to([r, b - a, 2, RD]),
                           ALU.mult).then_inc(ro_read, 1)
                    drain()

                def ret_squares(c):
                    for i, (r, a, b) in enumerate(parts):
                        sq = rsq[0:r, i, 0:(b - a) * P].rearrange("p (t h d) -> p t h d", h=2, d=RD)
                        TT(sq, heads(ort, r, a, b, c), heads(ort, r, a, b, c), ALU.mult)
                    drain()
                    ss = small[:, 52:72].rearrange("p (t h) -> p t h", t=NT)
                    for i, (r, a, b) in enumerate(parts):
                        sq = rsq[0:r, i, 0:(b - a) * P].rearrange("p (t h d) -> p t h d", h=2, d=RD)
                        nc.vector.tensor_reduce(ss[0:r, a:b, 2 * c:2 * c + 2], sq, AX, ALU.add)

                def ret_mask(h):
                    dve.wait_ge(rs_read, l * 16 + 4 * h + 4)
                    for j, (t0, R) in enumerate(TB):
                        o = SC_OFF[j]
                        TT(sc[0:R, h % 2, o:o + R], sc[0:R, h % 2, o:o + R], C("keep", R)[:, 0:R], ALU.mult)
                    drain()
                    dve.sem_inc(rs_mask, 1)

                scaled(N_IN - 1, btile[1][:, :])
                freed()
                conv_out(1)
                ret_mask(0)
                for i in LOADS[N_IN - 1]:
                    low(l, i)
                conv_low(1)
                ret_mask(1)
                ret_mask(2)
                ret_out(0)
                ret_squares(0)
                ret_mask(3)
                ret_out(1)
                ret_squares(1)
                drain()
                dve.sem_inc(ro_ss, 1)

                def biggest(u):
                    tt = u // NH
                    q0, R = TA[tt]
                    it = u if u < NH else u + 2
                    b = 4 + 2 * (it % 2)
                    dve.wait_ge(a_s, l * 40 + u + 1)
                    nc.vector.tensor_reduce(nmax[0:R, u:u + 1], psf[0:R, b * 512:b * 512 + q0 + R], AX, ALU.max,
                                            negate=True).then_inc(a_max, 1)

                def ptm_read(u):
                    R = TA[u // NH][1]
                    dve.wait_ge(a_tr, l * 40 + u + 1)
                    if u >= 2:
                        dve.wait_ge(a_pv, l * 40 + u - 1)
                    copy(ptm[0:META, u % 2, 0:R], meta_keys(u)).then_inc(a_ptm, 1)

                def normalised(tt):
                    R = TA[tt][1]
                    dve.wait_ge(a_pv, l * 40 + tt * NH + NH)
                    nc.vector.reciprocal(esum[0:R, tt * NH:(tt + 1) * NH], esum[0:R, tt * NH:(tt + 1) * NH])
                    drain()
                    if tt:
                        dve.wait_ge(a_ytr, l * NT + tt)
                    TT(yo[0:R, :].rearrange("p (h d) -> p h d", h=NH),
                       ps[0:R, o_bank(tt), :].rearrange("p (h d) -> p h d", h=NH),
                       esum[0:R, tt * NH:(tt + 1) * NH].unsqueeze(2).broadcast_to([R, NH, DV]),
                       ALU.mult).then_inc(a_o, 1)

                def y_low(tt):
                    t0, R = TA[tt]
                    dve.wait_ge(ya_hi, l * NT + tt + 1)
                    TT(yl[:, 4:8, t0:t0 + R], ps[:, o_bank(tt), :].rearrange("p (f t) -> p f t", f=4)[:, :, 0:R],
                       yh[:, 4:8, t0:t0 + R].bitcast(F32), ALU.subtract).then_inc(ya_lo, 1)

                for u in range(41):
                    if u < 40:
                        biggest(u)
                    if u == 2:
                        dve.wait_ge(ro_std, l + 1)
                        nc.vector.reciprocal(small[:, 32:52], small[:, 32:52])
                        drain()
                        scale = small[:, 32:52].rearrange("p (t h) -> p t h", t=NT)
                        for r, a, b in parts:
                            o = ort[0:r, a:b, :].rearrange("p t (h d) -> p t h d", h=RH)
                            TT(o, o, scale[0:r, a:b, :].unsqueeze(3).broadcast_to([r, b - a, RH, RD]), ALU.mult)
                        drain()
                        dve.sem_inc(ro_tok, 1)
                    if u >= 1:
                        v = u - 1
                        if v >= NH and v % 2 == 0:
                            pt_read(dve, None, l, v)
                        ptm_read(v)
                    if u == 7:
                        dve.wait_ge(gate_new, l * 2 + 2)
                        for f in range(2):
                            dve.wait_ge(ry_tr, l * 2 + f + 1)
                            o = (4 + 2 * f) * 512
                            STT(gate[:, f, :], psf[:, o:o + T], PAR("ret_g", f), gate[:, f, :], ALU.mult,
                                ALU.mult).then_inc(yr_new, 1)
                    if u == 12:
                        for f in range(2):
                            dve.wait_ge(yr_hi, l * 2 + f + 1)
                            TT(yl[:, 2 + f, :], gate[:, f, :], yh[:, 2 + f, :].bitcast(F32),
                               ALU.subtract).then_inc(yr_lo, 1)
                    if u % NH == 1 and u > NH:
                        normalised(u // NH - 1)
                    if u % NH == 6 and u > NH:
                        y_low(u // NH - 1)
                normalised(NT - 1)
                y_low(NT - 1)

                for n in range(N_IN, PRE_TILES):
                    k = n - N_IN
                    x_add(k, n, tile_no(l, n), xm_new)
                    if n in LOADS:
                        for i in LOADS[n]:
                            low(l, i)
                    else:
                        mlp_low(l, 0, n - 22)
                    x_low("mlp_g", k, xm_hi, xm_lo, l * KT + k + 1)

                group(l, 0, "first")
                with dve.Fori(1, NGRP - 1) as g:
                    group(l, g, "middle")
                group(l, NGRP - 1, "last")

            for i in range(0, 8, 2):
                dve.wait_ge(fin_tr, i + 1)
                if i:
                    dve.wait_ge(fin_read, i)
                copy(xout[:, i // 2, 0:512], ps[:, i % 4, :]).then_inc(fin_read, 1)

        @block.gpsimd
        def _(pool):
            def squares(sem_new, value, sem_sq, reads):
                for k in range(KT):
                    pool.wait_ge(sem_new, value + k + 1)
                    if k == 0:
                        if reads is not None:
                            pool.wait_ge(ms_done, reads)
                        nc.gpsimd.tensor_tensor(acc[:, :], xT[:, 0, :], xT[:, 0, :], ALU.mult)
                        continue
                    nc.gpsimd.tensor_tensor(sqx[:, :], xT[:, k, :], xT[:, k, :], ALU.mult)
                    nc.gpsimd.drain()
                    last = nc.gpsimd.tensor_tensor(acc[:, :], acc[:, :], sqx[:, :], ALU.add)
                    if k < KT - 1:
                        nc.gpsimd.drain()
                last.then_inc(sem_sq, 1)

            squares(xa_new, 0, xa_sq, None)
            with pool.Fori(0, DEPTH) as l:
                squares(xm_new, l * KT, xm_sq, 2 * l + 1)
                squares(xa_new, (l + 1) * KT, xa_sq, 2 * l + 2)


def constants():
    import numpy as np
    f = np.float32
    c = np.zeros((P, N_CONST), f)

    def put(name, a):
        o, w = CONSTS[name]
        c[:, o:o + w] = a

    p = np.arange(P)
    put("ident", np.eye(P, dtype=f))
    put("perm", (p[:, None] == (p ^ 32)[None, :]).astype(f))
    put("ones", 1.0)
    put("keep", (p[None, :] >= p[:, None]).astype(f))

    def angles(dim):
        inv = f(1.0) / (f(10000.0) ** (np.arange(0, dim, 2, dtype=f) / f(dim)))
        ang = np.arange(T, dtype=f)[:, None] * inv[None, :]
        return np.cos(ang).astype(f), np.sin(ang).astype(f)

    cr, sr = angles(RD)
    half = RD // 2
    put("rope_c", cr.T[p % half])
    put("rope_s", sr.T[p % half] * np.where(p % RD < half, -1, 1)[:, None])
    cm, sm = angles(ROPE)
    tc, ts = np.zeros((P, NT, ROPE), f), np.zeros((P, NT, ROPE), f)
    for t, (t0, n) in enumerate(TA):
        tc[:n, t] = np.concatenate([cm[t0:t0 + n], cm[t0:t0 + n]], 1)
        ts[:n, t] = np.concatenate([-sm[t0:t0 + n], sm[t0:t0 + n]], 1)
    put("tok_c", tc.reshape(P, -1))
    put("tok_s", ts.reshape(P, -1))
    log_g = np.log1p(-np.exp2(-5.0 - np.arange(RH)))
    pos = (p[:, None] + P * np.arange(NT)[None, :])[:, :, None] * log_g
    put("g_out", np.exp(pos).reshape(P, -1))
    put("g_in", (np.exp(-pos) * RD ** -0.5).reshape(P, -1))
    put("eps", EPS)
    put("eps_q", QK * EPS)
    mask = np.where(p[None, :] <= p[:, None], 0.0, NEG).astype(f)
    return c, mask


def kernel(x, meta_tokens, attn_norm_g, w_in, conv_w, ret_gn_g, q_norm_g, w_uq, kv_norm_g, w_ukv,
           q_head_norm_g, k_head_norm_g, w_out, mlp_norm_g, w_mlp_in, w_mlp_out):
    import numpy as np
    import concourse.bacc as bacc
    from concourse.bass_utils import run_bass_kernel_spmd as run

    con, mask = constants()
    par = np.ones((DEPTH + 1, P, N_PARAM), np.float32)

    def put(name, a):
        o, w = PARAMS[name]
        par[:DEPTH, :a.shape[1], o:o + w] = a

    put("attn_g", np.asarray(attn_norm_g).reshape(DEPTH, KT, P).transpose(0, 2, 1))
    put("mlp_g", np.asarray(mlp_norm_g).reshape(DEPTH, KT, P).transpose(0, 2, 1))
    put("qn_g", np.asarray(q_norm_g).reshape(DEPTH, 2, P).transpose(0, 2, 1))
    put("kvn_g", np.asarray(kv_norm_g).reshape(DEPTH, P, 1))
    put("conv", np.asarray(conv_w).reshape(DEPTH, 3, 2, P).transpose(0, 3, 2, 1).reshape(DEPTH, P, 6))
    put("ret_g", np.asarray(ret_gn_g).reshape(DEPTH, 2, P).transpose(0, 2, 1))
    put("qh_g", np.asarray(q_head_norm_g)[:, :NOPE, None])
    put("kh_g", np.asarray(k_head_norm_g)[:, :NOPE, None])
    put("qrope_g", np.broadcast_to(np.asarray(q_head_norm_g)[:, None, NOPE:], (DEPTH, P, ROPE)))
    put("krope_g", np.broadcast_to(np.asarray(k_head_norm_g)[:, None, NOPE:], (DEPTH, P, ROPE)))
    par[DEPTH] = par[DEPTH - 1]

    nc = bacc.Bacc("TRN2", target_bir_lowering=False, num_devices=1)
    arrays = {"x": x, "meta": meta_tokens, "consts": con, "maskneg": mask, "params": par, "w_in": w_in,
              "w_uq": w_uq, "w_ukv": w_ukv, "w_out": w_out, "w_mlp_in": w_mlp_in, "w_mlp_out": w_mlp_out}
    arrays = {f"{n}_dram": np.ascontiguousarray(a) for n, a in arrays.items()}
    args = [nc.dram_tensor(n, a.shape, mybir.dt.from_np(a.dtype), kind="ExternalInput").ap()
            for n, a in arrays.items()]
    out = nc.dram_tensor("out_dram", (1, SEQ, D), F32, kind="ExternalOutput").ap()
    trunk(nc, *args, out)
    return run(nc, [arrays], core_ids=[0]).results[0]["out_dram"]
```

```python
from contextlib import ExitStack

import concourse.bass as bass
from concourse import mybir

F32 = mybir.dt.float32
F32R = mybir.dt.float32r
BF16 = mybir.dt.bfloat16
ALU = mybir.AluOpType
ACT = mybir.ActivationFunctionType
AX = mybir.AxisListType.X

P = 128
DEPTH, D, SEQ, META = 2, 1024, 512, 16
T = META + SEQ
TH = T // 2
KT = D // P
EPS = 1e-6
CONV_W = 256
RH, RD = 4, 64
NH, NOPE, ROPE, DV = 8, 64, 32, 64
QK = NOPE + ROPE
HG = NH // 2
Q_LORA, KV_LORA = 256, 128
DFF = 4 * D
FG = 1024
NGRP = DFF // FG
NT = 5

OFF_B, OFF_C, OFF_H = 0, 256, 512
OFF_RQ, OFF_RK, OFF_RV, OFF_RG = 768, 1024, 1280, 1536
OFF_CQ, OFF_CKV = 1792, 2048
D_IN = 2208

TA = [(0, META)] + [(META + P * i, P) for i in range(NT - 1)]
TB = [(P * i, min(P, T - P * i)) for i in range(NT)]

N_IN, N_OUT = 18, 8
PRE_TILES = N_IN + N_OUT
GT = 16
L_TILES = PRE_TILES + GT * NGRP
PRE_HALVES = 32
L_HALVES = PRE_HALVES + GT * NGRP
PRE_BLOCKS = PRE_HALVES // 2
L_BLOCKS = L_HALVES // 2
WS = 4
SS = 2

HALVES = ([("T", n) for n in range(6)] + [("U", 0), ("U", 1)] + [("T", n) for n in range(6, 10)] + [("U", 2), ("U", 3)]
          + [("T", 10), ("T", 11)] + [("U", 4), ("U", 5)] + [("T", n) for n in range(12, PRE_TILES)])
TILE_HALF = {n: i for i, (kind, n) in enumerate(HALVES) if kind == "T"}
MLA_HALF = {n: i for i, (kind, n) in enumerate(HALVES) if kind == "U"}
SLOT = {}
for _n in range(PRE_TILES):
    SLOT[TILE_HALF[_n]] = _n % 4 if _n < 4 or _n >= 18 - 2 else _n % 2
for _n in range(18, PRE_TILES):
    SLOT[TILE_HALF[_n]] = (_n - 18) % 4
SLOT[TILE_HALF[16]], SLOT[TILE_HALF[17]] = 2, 3
for _n in range(6):
    SLOT[MLA_HALF[_n]] = 2 + _n % 2
LOADS = {0: [4], 1: [5], 2: [6], 3: [7], 4: [8], 5: [9], 6: [10], 7: [11, 12, 13], 8: [14], 9: [15, 16, 17],
         10: [18], 11: [19], 12: [20], 13: [21, 22, 23], 14: [24], 15: [25], 16: [26], 17: [27],
         18: [28], 19: [29], 20: [30], 21: [31]}
FREED = {4: ("T", 0), 5: ("T", 1), 6: ("T", 2), 7: ("T", 3), 8: ("T", 4), 9: ("T", 5), 10: ("T", 6), 11: ("T", 7),
         12: ("U", 4), 13: ("U", 4), 14: ("T", 8), 15: ("T", 9), 16: ("U", 9), 17: ("U", 9), 18: ("T", 10),
         19: ("T", 11), 20: ("T", 12), 21: ("T", 13), 22: ("U", 14), 23: ("U", 19), 24: ("T", 14), 25: ("T", 15),
         26: ("T", 16), 27: ("T", 17), 28: ("T", 18), 29: ("T", 19), 30: ("T", 20), 31: ("T", 21)}

GAPS = {n: [] for n in range(6, 15)}
_u = 0
_t = 0
for _gap, _cnt in zip(range(6, 15), [3, 2, 3, 2, 3, 2, 3, 2, 0]):
    GAPS[_gap] = [("tr", _t + _i) for _i in range(_u - _t)]
    _t = _u
    GAPS[_gap] += [("u", _u + _i) for _i in range(_cnt)]
    _u += _cnt
AUX_SEQ = [x for g in range(6, 15) for x in GAPS[g]]
AUX_BANK = {x: 4 + i % 4 for i, x in enumerate(AUX_SEQ)}
AUX_PREV = {x: (AUX_SEQ[i - 4] if i >= 4 else None) for i, x in enumerate(AUX_SEQ)}

CONSTS = {}
_c = 0
for _name, _w in (("ident", P), ("perm", P), ("ones", P), ("keep", P), ("rope_c", T), ("rope_s", T),
                  ("tok_c", NT * ROPE), ("tok_s", NT * ROPE), ("g_out", NT * RH), ("g_in", NT * RH),
                  ("eps", 1), ("eps_q", 1)):
    CONSTS[_name] = (_c, _w)
    _c += _w
N_CONST = _c
PARAMS = {}
_c = 0
for _name, _w in (("attn_g", KT), ("mlp_g", KT), ("qn_g", 2), ("kvn_g", 1), ("conv", 6), ("ret_g", 2),
                  ("qh_g", 1), ("kh_g", 1), ("qrope_g", ROPE), ("krope_g", ROPE)):
    PARAMS[_name] = (_c, _w)
    _c += _w
N_PARAM = _c
NEG = -1e30


def trunk(nc, x, meta, consts, maskneg, params, w_in, w_uq, w_ukv, w_out, w_mlp_in, w_mlp_out, out):
    with ExitStack() as ctx:
        at = [nc.sbuf_base + (-nc.sbuf_base) % 32]

        def own(name, shape, dt=F32):
            size = 4 if dt != BF16 else 2
            for s in shape[1:]:
                size *= s
            off = at[0]
            at[0] += size + (-size) % 32
            return nc.alloc_sbuf_tensor_at(name, shape, dt, offset=off), off

        def over(name, shape, off, dt=F32):
            return nc.alloc_sbuf_tensor_at(name, shape, dt, offset=off)

        def sem(name):
            return ctx.enter_context(nc.semaphore(name))

        TB4 = T * 4
        xT, _ = own("xT", [P, KT, T])
        hh, hreg = own("hh", [P, KT, T], F32R)
        hl, _ = own("hl", [P, KT, T], F32R)
        yh, yreg = own("yh", [P, KT, T], F32R)
        yl, _ = own("yl", [P, KT, T], F32R)
        stage, _ = own("stage", [P, SS, 2048])
        wh, _ = own("wh", [P, WS, 1024], F32R)
        wl, _ = own("wl", [P, WS, 1024], F32R)
        qT, qreg = own("qT", [P, NH, T])
        kT, kreg = own("kT", [P, NH, T])
        V, _ = own("V", [P, NT, NH * DV])
        con, _ = own("con", [P, N_CONST])
        par, _ = own("par", [P, N_PARAM])
        identb, _ = own("identb", [P, P], BF16)
        maskb, _ = own("maskb", [P, P], BF16)
        tabs, _ = own("tabs", [P, 4, NT, ROPE])
        acc, _ = own("acc", [P, T])
        sq0, sqreg = own("sq0", [P, T])
        tmp, tmpreg = own("tmp", [P, T])
        rstd, _ = own("rstd", [P, T])
        gate, _ = own("gate", [P, 2, T])
        raw, _ = own("raw", [P, 2, T])
        qn, _ = own("qn", [P, 3, HG * QK])
        rt, _ = own("rt", [P, 2, HG * ROPE])
        ust, _ = own("ust", [P, 20, HG])
        uss, _ = own("uss", [P, 3, HG])
        krg, _ = own("krg", [P, NT, ROPE])
        small, _ = own("small", [P, 72])
        assert at[0] <= nc.sbuf_usable_end, (at[0], nc.sbuf_usable_end)

        sq1 = over("sq1", [P, T], tmpreg)
        sqx = over("sqx", [P, T], sqreg)
        lo = yreg + KT * TB4
        ch, cl = over("ch", [P, 3, T], yreg, F32R), over("cl", [P, 3, T], lo, F32R)
        ckv = over("ckv", [P, T], yreg + 3 * TB4)
        cu = [over("cu0", [P, T], yreg + 3 * TB4), over("cu1", [P, T], lo + 4 * TB4 + NT * RH * RD * 4)]
        kr = over("kr", [P, NT, ROPE], lo + 5 * TB4 + NT * RH * RD * 4)
        cacc = [over("ca0", [P, T], lo + 2 * TB4), over("ca1", [P, T], lo + 3 * TB4)]
        rqk = over("rqk", [P, 4, T], yreg + 4 * TB4)
        vtok = over("vtok", [P, NT, RH * RD], lo + 4 * TB4)
        krT = over("krT", [P, T], kreg)
        hoff = [hreg]

        def over_h(name, shape):
            size = 4
            for s in shape[1:]:
                size *= s
            t = over(name, shape, hoff[0])
            hoff[0] += size + (-size) % 32
            assert hoff[0] <= hreg + 2 * KT * TB4
            return t

        SC_OFF = [0, 528, 928, 1200, 1344]
        sc_odd = over_h("sc_odd", [P, 1360])
        ort = over_h("ort", [P, NT, RH * RD])
        pb = over_h("pb", [P, 3, T])
        pt = over_h("pt", [P, 3, 512])
        ptm = over_h("ptm", [P, 2, P])
        yo = over_h("yo", [P, NH * DV])
        nmax = over_h("nmax", [P, NT * NH])
        esum = over_h("esum", [P, NT * NH])

        def sc(h, j, rows, a, b):
            part, o = min(j, 2), SC_OFF[j] - SC_OFF[min(j, 2)]
            if h % 2 == 0:
                return [raw[0:rows, 0, :], raw[0:rows, 1, :], cu[0][0:rows, :]][part][:, o + a:o + b]
            return sc_odd[0:rows, SC_OFF[j] + a:SC_OFF[j] + b]

        tb = over("tb", [P, 2, T], qreg)
        ts = over("ts", [P, 2, T], qreg + 2 * TB4)
        xin = over("xin", [P, 4, D], qreg)
        xmeta = over("xmeta", [P, D], kreg)
        mneg = over("mneg", [P, P], kreg + 4 * D)
        xout = over("xout", [P, 4, D], qreg)

        ps = ctx.enter_context(nc.psum_tensor("ps", [P, 8, 512], F32))
        psf = ps[:, :, :].rearrange("p b c -> p (b c)")

        def C(name, rows=P):
            o, w = CONSTS[name]
            return con[0:rows, o:o + w]

        def PAR(name, i=0, rows=P):
            o, _ = PARAMS[name]
            return par[0:rows, o + i:o + i + 1]

        def pair(b):
            return ps[:, b:b + 2, 0:TH]

        def two(ap):
            return ap.rearrange("p (a b) -> p a b", a=2)

        def query(turn):
            return NT - 1 - turn

        def s_bank(u):
            return 4 + 2 * (u % 2)

        def o_bank(turn):
            return 3 - turn % 2

        def meta_keys(u):
            if query(u // NH) == 0:
                return ps[0:META, u % 2, 0:META]
            return ps[0:META, s_bank(u) + 1, META:META + P]

        ident = C("ident")
        lat_sq = [sq0, tmp, acc]
        btile = [sq0, tmp]

        con_in = sem("con_in")
        settled = sem("settled")
        ident_in = sem("ident_in")
        x_in = [sem("x_in0"), sem("x_in1")]
        par_in = sem("par_in")
        stage_in = [sem(f"stage_in{i}") for i in range(SS)]
        w_hi = sem("w_hi")
        w_lo = sem("w_lo")
        t_done = sem("t_done")
        t_read = sem("t_read")
        xt_done = sem("xt_done")
        xt_read = sem("xt_read")
        xa_new, xa_hi, xa_lo, xa_sq = sem("xa_new"), sem("xa_hi"), sem("xa_lo"), sem("xa_sq")
        xm_new, xm_hi, xm_lo, xm_sq = sem("xm_new"), sem("xm_hi"), sem("xm_lo"), sem("xm_sq")
        ms_done = sem("ms_done")
        std_new = sem("std_new")
        s_new, s_hi, s_lo = sem("s_new"), sem("s_hi"), sem("s_lo")
        tabs_new = sem("tabs_new")
        raw_new, raw_sq, raw_ms = sem("raw_new"), sem("raw_sq"), sem("raw_ms")
        lat_std, lat_new, lat_hi, lat_lo = sem("lat_std"), sem("lat_new"), sem("lat_hi"), sem("lat_lo")
        kr_tr, kr_read, kr_ss = sem("kr_tr"), sem("kr_read"), sem("kr_ss")
        u_done, u_sq, u_ss, u_std, u_read, u_tok = (sem("u_done"), sem("u_sq"), sem("u_ss"), sem("u_std"),
                                                    sem("u_read"), sem("u_tok"))
        tr_done, tr_read = sem("tr_done"), sem("tr_read")
        rq_new, rp_done, rp_read = sem("rq_new"), sem("rp_done"), sem("rp_read")
        rv_tr, rv_read = sem("rv_tr"), sem("rv_read")
        gz_new, gate_new = sem("gz_new"), sem("gate_new")
        yc_new, yc_hi, yc_lo = sem("yc_new"), sem("yc_hi"), sem("yc_lo")
        rs_done, rs_read, rs_diag, ro_done, ro_read, ro_ss, ro_std, ro_tok, ry_tr, yr_new, yr_hi, yr_lo = (
            sem(n) for n in ("rs_done", "rs_read", "rs_diag", "ro_done", "ro_read", "ro_ss", "ro_std", "ro_tok",
                             "ry_tr", "yr_new", "yr_hi", "yr_lo"))
        a_s, a_max, a_exp, a_tr, a_pt, a_ptm, a_pv, a_o, a_ytr, ya_hi, ya_lo = (
            sem(n) for n in ("a_s", "a_max", "a_exp", "a_tr", "a_pt", "a_ptm", "a_pv", "a_o", "a_ytr",
                             "ya_hi", "ya_lo"))
        fin_tr, fin_read, out_done = sem("fin_tr"), sem("fin_read"), sem("out_done")

        def settle(eng):
            eng.sem_inc(settled, 1)

        def tile_no(l, n):
            return (l + 1) * L_TILES + n + 1

        def half_no(l, i):
            return l * L_HALVES + i + 1

        W_PRIME = 2

        def grp(l, g, n, per=GT):
            return l * 0 + (l * NGRP + g) * per + n + 1

        block = ctx.enter_context(nc.Block())

        @block.sync
        def _(sp):
            sp.dma_start(con[:, 0:P], consts[:, 0:P]).then_inc(ident_in, 16)
            sp.dma_start(xmeta[0:META, :], meta).then_inc(x_in[0], 16)
            x3 = x[0].rearrange("(t p) d -> p t d", p=P)
            sp.dma_start(xin[:, :, 0:D // 2], x3[:, :, 0:D // 2]).then_inc(x_in[0], 16)
            sp.dma_start(par[:, :], params[0]).then_inc(par_in, 16)
            sp.dma_start(xin[:, :, D // 2:D], x3[:, :, D // 2:D]).then_inc(x_in[1], 16)

            def load(l, j, dst, src):
                sp.wait_ge(w_lo, W_PRIME + l * L_HALVES + 2 * (j - 1))
                settle(sp)
                sp.dma_start(dst, src).then_inc(stage_in[j % SS], 16)

            def slab(j, w=256):
                return stage[:, j % SS, 0:KT * w].rearrange("p (k n) -> p k n", k=KT)

            def first_loads(l, source):
                for j, (col, w) in enumerate(((OFF_CQ, 256), (OFF_CKV, 160))):
                    load(l, j, slab(j, w), w_in[source, :, col:col + w].rearrange("(k p) n -> p k n", p=P))

            first_loads(0, 0)
            sp.dma_start(con[:, P:N_CONST], consts[:, P:N_CONST]).then_inc(con_in, 16)
            sp.dma_start(mneg[:, :], maskneg).then_inc(con_in, 16)
            with sp.Fori(0, DEPTH) as l:
                def win(col, w=256):
                    return w_in[l, :, col:col + w].rearrange("(k p) n -> p k n", p=P)

                def uq(c):
                    return w_uq[l, :, c * HG * QK:(c + 1) * HG * QK].rearrange("(k p) n -> p k n", p=P)

                load(l, 2, slab(2), win(OFF_RQ))
                load(l, 3, stage[:, 1, 0:2 * HG * QK].rearrange("p (k n) -> p k n", k=2), uq(0))
                load(l, 4, slab(4), win(OFF_RK))
                load(l, 5, slab(5), win(OFF_RV))
                load(l, 6, stage[:, 0, 0:2 * HG * QK].rearrange("p (k n) -> p k n", k=2), uq(1))
                load(l, 7, slab(7), win(OFF_RG))
                load(l, 8, stage[:, 0, 0:1024], w_ukv[l])
                for j, col in ((9, OFF_C), (10, OFF_H), (11, OFF_B)):
                    load(l, j, slab(j), win(col))
                for c in range(4):
                    load(l, 12 + c, slab(12 + c),
                         w_out[l, :, c * 256:(c + 1) * 256].rearrange("(k p) n -> p k n", p=P))

                def group(g):
                    for c in range(4):
                        sp.wait_ge(w_lo, W_PRIME + l * L_HALVES + PRE_HALVES + g * GT + 2 * (c - 1))
                        settle(sp)
                        sp.dma_start(slab(c), w_mlp_in[l, :, bass.ds(g * FG + c * 256, 256)]
                                     .rearrange("(k p) n -> p k n", p=P)).then_inc(stage_in[c % SS], 16)
                    for c in range(4):
                        sp.wait_ge(w_lo, W_PRIME + l * L_HALVES + PRE_HALVES + g * GT + 2 * (c + 3))
                        settle(sp)
                        sp.dma_start(slab(c), w_mlp_out[l, bass.ds(g * FG, FG), c * 256:(c + 1) * 256]
                                     .rearrange("(k p) n -> p k n", p=P)).then_inc(stage_in[c % SS], 16)

                group(0)
                sp.wait_ge(xm_lo, l * KT + KT)
                settle(sp)
                sp.dma_start(par[:, :], params[l + 1]).then_inc(par_in, 16)
                with sp.Fori(1, NGRP - 1) as g:
                    group(g)
                group(NGRP - 1)
                first_loads(l + 1, (l + 1) % DEPTH)

            for t in range(4):
                sp.wait_ge(fin_read, 2 * t + 2)
                sp.dma_start(out[0, t * P:(t + 1) * P, :], xout[:, t, :]).then_inc(out_done, 16)
            sp.wait_ge(out_done, 16 * 4)

        @block.tensor
        def _(pe):
            mm = nc.tensor.matmul
            pe.sem_inc(t_done, L_TILES)
            pe.wait_ge(ident_in, 16)
            for k in range(KT):
                b = 2 * (k % 2)
                if k == 0:
                    pe.wait_ge(x_in[0], 32)
                if k == KT // 2:
                    pe.wait_ge(x_in[1], 16)
                if k >= 2:
                    pe.wait_ge(xt_read, k - 1)
                nc.tensor.transpose(ps[:, b + 1, 0:META], xmeta[0:META, k * P:(k + 1) * P], ident[0:META, 0:META])
                for t in range(4):
                    last = nc.tensor.transpose(ps[:, b, t * P:(t + 1) * P], xin[:, t, k * P:(k + 1) * P], ident)
                last.then_inc(xt_done, 1)
            pe.wait_ge(con_in, 32)

            def gemm(no, slot, rh, rl, ready, order=range(KT)):
                b = 2 * (no % 2)
                for k in order:
                    if ready:
                        ready(k)
                    for w, r in ((wh, rh), (wh, rl), (wl, rh)):
                        for c in range(2):
                            last = mm(ps[:, b + c, 0:TH], w[:, slot, k * P:(k + 1) * P],
                                      r[:, k, c * TH:(c + 1) * TH],
                                      start=(k == order[0] and w is wh and r is rh),
                                      stop=(k == order[-1] and w is wl))
                return last

            def tile(l, n, rh, rl, ready=None, order=range(KT)):
                pe.wait_ge(w_lo, W_PRIME + half_no(l, TILE_HALF[n]))
                pe.wait_ge(t_read, tile_no(l, n - 2))
                gemm(n, SLOT[TILE_HALF[n]], rh, rl, ready, order).then_inc(t_done, 1)

            def mean_square(first_bank):
                for c in range(2):
                    last = mm(ps[:, first_bank + c, 0:TH], C("ones"), acc[:, c * TH:(c + 1) * TH],
                              start=True, stop=True)
                last.then_inc(ms_done, 1)

            def group(l, g, kind):
                for m in range(GT):
                    pe.wait_ge(w_lo, W_PRIME + l * L_HALVES + PRE_HALVES + g * GT + m + 1)
                    pe.wait_ge(t_read, (l + 1) * L_TILES + PRE_TILES + g * GT + m - 1)
                    if m < 8:
                        def ready(k):
                            if kind == "first" and m == 0:
                                pe.wait_ge(xm_lo, l * KT + k + 1)
                        gemm(m, m % WS, hh, hl, ready).then_inc(t_done, 1)
                        if kind == "first" and m == 0:
                            pe.wait_ge(xm_sq, l + 1)
                            mean_square(4)
                    else:
                        def ready(k):
                            if m == 8:
                                pe.wait_ge(s_lo, (l * NGRP + g) * 8 + k + 1)
                        gemm(m, m % WS, yh, yl, ready).then_inc(t_done, 1)

            with pe.Fori(0, DEPTH) as l:
                def aux_free(item):
                    prev = AUX_PREV[item]
                    if prev is not None:
                        kind, i = prev
                        pe.wait_ge(u_read if kind == "u" else tr_read, l * 20 + i + 1)

                def unit(u):
                    b = AUX_BANK[("u", u)]
                    aux_free(("u", u))
                    c, tt = u // NT % 2, u % NT
                    t0 = TA[tt][0]
                    if u < 10:
                        if u == 0:
                            pe.wait_ge(lat_lo, l * 3 + 2)
                        if tt == 0:
                            pe.wait_ge(w_lo, W_PRIME + half_no(l, MLA_HALF[2 * c + 1]))
                        for k in range(2):
                            s = SLOT[MLA_HALF[2 * c + k]]
                            for a, w in ((ch, wh), (cl, wh), (ch, wl)):
                                last = mm(ps[:, b, 0:HG * QK], a[:, k, t0:t0 + P], w[:, s, 0:HG * QK],
                                          start=(k == 0 and a is ch and w is wh), stop=(k == 1 and w is wl))
                    else:
                        if u == 10:
                            pe.wait_ge(lat_lo, l * 3 + 3)
                        if tt == 0:
                            pe.wait_ge(w_lo, W_PRIME + half_no(l, MLA_HALF[4 + c]))
                        s = SLOT[MLA_HALF[4 + c]]
                        for a, w in ((ch, wh), (cl, wh), (ch, wl)):
                            last = mm(ps[:, b, :], a[:, 2, t0:t0 + P], w[:, s, 0:512],
                                      start=(a is ch and w is wh), stop=(w is wl))
                    last.then_inc(u_done, 1)

                def unit_transpose(u):
                    b = AUX_BANK[("tr", u)]
                    aux_free(("tr", u))
                    R = TA[u % NT][1]
                    pe.wait_ge(u_tok, l * 20 + u + 1)
                    settle(pe)
                    for h in range(HG):
                        last = nc.tensor.transpose(ps[0:QK, b, h * P:h * P + R],
                                                   qn[0:R, u % 3, h * QK:(h + 1) * QK], ident[0:R, 0:R])
                    last.then_inc(tr_done, 1)

                def gap(n):
                    for kind, i in GAPS.get(n, []):
                        (unit if kind == "u" else unit_transpose)(i)

                def swap_halves(i):
                    b = 4 + 2 * (i % 2)
                    pe.wait_ge(rq_new, l * 4 + i + 1)
                    if i >= 2:
                        pe.wait_ge(rp_read, l * 4 + i - 1)
                    for c in range(2):
                        last = mm(ps[:, b + c, 0:TH], C("perm"), rqk[:, i, c * TH:(c + 1) * TH],
                                  start=True, stop=True)
                    last.then_inc(rp_done, 1)

                def ret_scores(h):
                    f, r = h // 2, RD * (h % 2)
                    kk, qq = rqk[r:r + RD, 2 + f, :], rqk[r:r + RD, f, :]
                    if h == 0:
                        pe.wait_ge(rv_read, l + 1)
                        pe.wait_ge(rp_read, l * 4 + 4)
                    if h >= 1:
                        pe.wait_ge(rs_read, l * 8 + 2 * h - 1)
                    for c in range(2):
                        last = mm(ps[:, 4 + c, 0:TH], kk[:, 0:P], qq[:, c * TH:(c + 1) * TH], start=True, stop=True)
                    last.then_inc(rs_done, 1)
                    if h >= 1:
                        pe.wait_ge(rs_read, l * 8 + 2 * h)
                    mm(ps[:, 6, 0:T - P], kk[:, P:2 * P], qq[:, P:T], start=True, stop=True).then_inc(rs_done, 1)
                    if h >= 1:
                        pe.wait_ge(rs_diag, l * 28 + 7 * h)
                    o = 0
                    for j in (2, 3, 4):
                        j0, R = TB[j]
                        last = mm(ps[0:R, 7, o:o + T - j0], kk[:, j0:j0 + R], qq[:, j0:T], start=True, stop=True)
                        o += T - j0
                    last.then_inc(rs_done, 1)

                for n in range(N_IN):
                    def ready(k):
                        if n == 0:
                            pe.wait_ge(xa_lo, l * KT + k + 1)
                        if n == N_IN - 1 and k == 5:
                            ret_scores(0)
                    tile(l, n, hh, hl, ready)
                    if n == 0:
                        pe.wait_ge(xa_sq, l + 1)
                        mean_square(4)
                    if n == 4:
                        for i, ks in ((0, (0, 1)), (1, (2,))):
                            b = 6 if i == 0 else 4
                            if i == 1:
                                pe.wait_ge(std_new, 2 * l + 1)
                            for k in ks:
                                pe.wait_ge(raw_sq, l * 3 + k + 1)
                                for c in range(2):
                                    last = mm(ps[:, b + c, 0:TH], C("ones"),
                                              lat_sq[k][:, c * TH:(c + 1) * TH],
                                              start=(k == ks[0]), stop=(k == ks[-1]))
                            last.then_inc(raw_ms, 1)
                    if n == 5:
                        pe.wait_ge(lat_std, l * 2 + 1)
                        pe.wait_ge(raw_new, l * 4 + 4)
                        settle(pe)
                        for tt, (t0, R) in enumerate(TA):
                            last = nc.tensor.transpose(ps[0:R, 6, tt * ROPE:(tt + 1) * ROPE],
                                                       krT[96:P, t0:t0 + R], ident[96:P, 96:P])
                        last.then_inc(kr_tr, 1)
                    if n == 6:
                        pe.wait_ge(lat_std, l * 2 + 2)
                        pe.wait_ge(kr_read, l + 1)
                    gap(n)
                    if n == 14:
                        pe.wait_ge(tr_read, l * 20 + 20)
                        swap_halves(0)
                        swap_halves(1)
                    if n == 15:
                        swap_halves(2)
                        swap_halves(3)
                    if n == 16:
                        pe.wait_ge(gz_new, l * 4 + 2)
                        pe.wait_ge(rp_read, l * 4 + 4)
                        for it, (t0, R) in enumerate(TB):
                            for f in range(2):
                                o = (it % 2) * 256 + f * P
                                last = nc.tensor.transpose(ps[0:R, 4 + it // 2, o:o + P],
                                                           raw[:, f, t0:t0 + R], ident)
                        last.then_inc(rv_tr, 1)

                def ret_sum(h):
                    pe.wait_ge(rs_read, l * 8 + 2 * h + 2)
                    pe.wait_ge(rs_diag, l * 28 + 7 * h + 7)
                    if h % 2 == 0:
                        pe.wait_ge(t_read, tile_no(l, N_IN - 2 + h // 2))
                    for it, (i0, R) in enumerate(TB):
                        for jt in range(it + 1):
                            j0, K = TB[jt]
                            b, o2 = 2 * (h // 2) + it // 4, (it % 4) * P + (h % 2) * RD
                            last = mm(ps[0:R, b, o2:o2 + RD],
                                      sc(h, jt, K, i0 - j0, i0 - j0 + R), vtok[0:K, jt, h * RD:(h + 1) * RD],
                                      start=(jt == 0), stop=(jt == it))
                    last.then_inc(ro_done, 1)

                ret_scores(1)
                ret_sum(0)
                ret_scores(2)
                ret_sum(1)
                ret_scores(3)
                ret_sum(2)

                def scores(u):
                    tt, h = query(u // NH), u % NH
                    q0, R = TA[tt]
                    L = q0 + R
                    b = s_bank(u)
                    if u < 2:
                        pe.wait_ge(rs_read, l * 8 + 8)
                        pe.wait_ge(rs_diag, l * 28 + 28)
                    else:
                        pe.wait_ge(a_exp, l * 40 + u - 1)
                    if u == 0:
                        pe.wait_ge(tr_read, l * 20 + 20)
                    n0 = min(L, 512)
                    q = qT[0:QK, h, q0:q0 + R]
                    pieces = [(0, n0)] + ([(512, L)] if L > 512 else [])
                    d0 = q0 if tt else 0
                    for i, (c0, c1) in enumerate(pieces):
                        if i and u >= 2:
                            pe.wait_ge(a_ptm, l * 40 + u - 1)
                        mm(psf[0:R, b * 512 + c0:b * 512 + c1], q, kT[0:QK, h, c0:c1], start=True, stop=False)
                        m0 = max(c0, d0)
                        last = mm(psf[0:R, b * 512 + m0:b * 512 + c1], identb[0:R, 0:R],
                                  maskb[0:R, m0 - d0:c1 - d0], start=False, stop=True)
                    last.then_inc(a_s, 1)

                def p_transpose(u):
                    tt, h = query(u // NH), u % NH
                    R = TA[tt][1]
                    pe.wait_ge(a_exp, l * 40 + u + 1)
                    if u == 0:
                        pe.wait_ge(ro_read, l * 4 + 2)
                    if u >= 2:
                        pe.wait_ge(a_ptm, l * 40 + u - 1)
                    if 2 <= u < 34:
                        pe.wait_ge(a_pt, l * 32 + u - 1)
                    if tt:
                        for b in range(1, tt + 1):
                            nc.tensor.transpose(ps[:, u % 2, (b - 1) * P:b * P],
                                                pb[:, u % 3, META + (b - 1) * P:META + b * P], ident)
                    settle(pe)
                    nc.tensor.transpose(meta_keys(u), pb[0:R, u % 3, 0:META],
                                        ident[0:R, 0:R]).then_inc(a_tr, 1)

                def p_v(u):
                    tt, h = query(u // NH), u % NH
                    R = TA[tt][1]
                    pe.wait_ge(a_ptm, l * 40 + u + 1)
                    if tt:
                        pe.wait_ge(a_pt, l * 32 + u + 1)
                    if u == 0:
                        pe.wait_ge(ro_read, l * 4 + 3)
                    if u == NH:
                        pe.wait_ge(ro_read, l * 4 + 4)
                    turn = u // NH
                    if h == 0 and turn >= 2:
                        pe.wait_ge(ya_lo, l * NT + turn - 1)
                    settle(pe)
                    o = ps[0:R, o_bank(turn), h * DV:(h + 1) * DV]
                    last = mm(o, ptm[0:META, u % 2, 0:R], V[0:META, 0, h * DV:(h + 1) * DV],
                              start=True, stop=(tt == 0))
                    for b in range(1, tt + 1):
                        last = mm(o, pt[:, u % 3, (b - 1) * P:b * P], V[:, b, h * DV:(h + 1) * DV],
                                  start=False, stop=(b == tt))
                    last.then_inc(a_pv, 1)

                def y_transpose(turn):
                    R = TA[query(turn)][1]
                    pe.wait_ge(a_o, l * NT + turn + 1)
                    settle(pe)
                    for f in range(4):
                        last = nc.tensor.transpose(ps[:, o_bank(turn), f * P:f * P + R], yo[0:R, f * P:(f + 1) * P],
                                                   ident[0:R, 0:R])
                    last.then_inc(a_ytr, 1)

                scores(0)
                scores(1)
                ret_sum(3)
                for u in range(40):
                    p_transpose(u)
                    if u + 2 < 40:
                        scores(u + 2)
                    if u >= 1:
                        p_v(u - 1)
                    if u % NH == 3 and u > NH:
                        y_transpose(u // NH - 1)
                p_v(39)

                def ret_transpose(f):
                    pe.wait_ge(ro_tok, l + 1)
                    settle(pe)
                    for it, (t0, R) in enumerate(TB):
                        last = nc.tensor.transpose(psf[:, (4 + 2 * f) * 512 + t0:(4 + 2 * f) * 512 + t0 + R],
                                                   ort[0:R, it, f * P:(f + 1) * P], ident[0:R, 0:R])
                    last.then_inc(ry_tr, 1)

                for n in range(N_IN, PRE_TILES):
                    def ready(k):
                        if n == N_IN:
                            if k < 2:
                                pe.wait_ge(yc_lo, l * 2 + k + 1)
                            elif k < 4:
                                pe.wait_ge(yr_lo, l * 2 + k - 1)
                            elif k == 4:
                                y_transpose(NT - 1)
                                ret_transpose(0)
                                ret_transpose(1)
                                pe.wait_ge(ya_lo, l * NT + NT)
                    tile(l, n, yh, yl, ready, (0, 1, 4, 5, 6, 7, 2, 3) if n == N_IN else range(KT))

                group(l, 0, "first")
                with pe.Fori(1, NGRP - 1) as g:
                    group(l, g, "middle")
                group(l, NGRP - 1, "last")

            pe.wait_ge(xa_new, (DEPTH + 1) * KT)
            pe.wait_ge(t_read, (DEPTH + 1) * L_TILES)
            for t in range(4):
                for f in range(2):
                    i = 2 * t + f
                    if i >= 4:
                        pe.wait_ge(fin_read, i - 3)
                    for k in range(4):
                        last = nc.tensor.transpose(ps[:, i % 4, k * P:(k + 1) * P],
                                                   xT[:, 4 * f + k, META + t * P:META + (t + 1) * P], ident)
                    last.then_inc(fin_tr, 1)

        def pt_read(eng, copy, l, u):
            tt = query(u // NH)
            eng.wait_ge(a_tr, l * 40 + u + 1)
            if u >= 3:
                eng.wait_ge(a_pv, l * 40 + u - 2)
            src, dst = ps[:, u % 2, 0:tt * P], pt[:, u % 3, 0:tt * P]
            if u:
                eng.wait_ge(a_pt, l * 32 + u)
            if copy is None:
                nc.vector.tensor_copy(dst, src).then_inc(a_pt, 1)
            else:
                copy(dst, src, ACT.Copy).then_inc(a_pt, 1)

        def y_hi(act, A, l, turn):
            t0, R = TA[query(turn)]
            act.wait_ge(a_ytr, l * NT + turn + 1)
            A(yh[:, 4:8, t0:t0 + R], ps[:, o_bank(turn), :].rearrange("p (f t) -> p f t", f=4)[:, :, 0:R],
              ACT.Copy).then_inc(ya_hi, 1)

        @block.scalar
        def _(act):
            A = nc.scalar.activation
            act.wait_ge(par_in, 16)

            def x_split(g, k, sem_new, sem_hi, value):
                act.wait_ge(sem_new, value)
                A(hh[:, k, :], xT[:, k, :], ACT.Copy, scale=PAR(g, k)).then_inc(sem_hi, 1)


            def source(i):
                st = stage[:, (i // 2) % SS, :]
                h = i % 2
                if HALVES[i] == ("T", 2):
                    return st[:, 0:KT * 160].rearrange("p (k n) -> p k n", k=KT)[:, :, 0:P], KT
                if HALVES[i] == ("T", 3):
                    return st[:, 0:KT * 160].rearrange("p (k n) -> p k n", k=KT)[:, :, 32:160], KT
                if HALVES[i][0] == "T":
                    return st.rearrange("p (k n) -> p k n", k=KT)[:, :, h * P:(h + 1) * P], KT
                w = HG * QK if HALVES[i][1] < 4 else 512
                return st[:, h * w:(h + 1) * w], w

            def hi(l, i):
                src, n = source(i)
                dst = wh[:, SLOT[i], :].rearrange("p (k n) -> p k n", k=KT) if n == KT else wh[:, SLOT[i], 0:n]
                j = i // 2
                act.wait_ge(stage_in[j % SS], 16 * (l * (L_BLOCKS // 2) + j // 2 + 1))
                if i < 4:
                    act.wait_ge(t_done, tile_no(l, i - 4))
                else:
                    kind, n = FREED[i]
                    if kind == "T":
                        act.wait_ge(t_done, tile_no(l, n))
                    else:
                        act.wait_ge(u_done, l * 20 + n + 1)
                A(dst, src, ACT.Copy).then_inc(w_hi, 1)

            def mlp_hi(l, g, m, freed):
                j = m // 2
                act.wait_ge(stage_in[j % SS], 16 * (l * (L_BLOCKS // 2) + PRE_BLOCKS // 2 + g * 4 + j // 2 + 1))
                act.wait_ge(t_done, freed)
                A(wh[:, m % WS, :].rearrange("p (k n) -> p k n", k=KT),
                  stage[:, j % SS, :].rearrange("p (k n) -> p k n", k=KT)[:, :, (m % 2) * P:(m % 2 + 1) * P],
                  ACT.Copy).then_inc(w_hi, 1)

            def root(value):
                act.wait_ge(ms_done, value)
                A(two(tmp[:, :]), pair(4), ACT.Sqrt, bias=C("eps"), scale=1.0 / D).then_inc(std_new, 1)

            def group(l, g, kind):
                for m in range(GT):
                    if kind != "last" or m < GT - 4:
                        mlp_hi(l, g if m < GT - 4 else g + 1, (m + 4) % GT,
                               (l + 1) * L_TILES + PRE_TILES + g * GT + m + 1)
                    else:
                        hi(l + 1, m - (GT - 4))
                    if kind == "first" and m == 0:
                        root(2 * l + 2)
                    if m < 8:
                        act.wait_ge(s_new, (l * NGRP + g) * 8 + m + 1)
                        A(yh[:, m, :], ts[:, m % 2, :], ACT.Copy).then_inc(s_hi, 1)
                    elif kind == "last":
                        if m == 8:
                            act.wait_ge(par_in, 16 * (l + 2))
                        x_split("attn_g", m - 8, xa_new, xa_hi, (l + 1) * KT + m - 7)

            for k in range(KT):
                if k == KT - 2:
                    hi(0, 0)
                x_split("attn_g", k, xa_new, xa_hi, k + 1)
            for i in range(1, 4):
                hi(0, i)
            act.wait_ge(con_in, 32)
            with act.Fori(0, DEPTH) as l:
                def unit(u):
                    b = AUX_BANK[("u", u)]
                    c, tt = u // NT % 2, u % NT
                    R = TA[tt][1]
                    s = [sq0, sq1][u % 2]
                    if u == 0:
                        act.wait_ge(kr_ss, l + 1)
                    act.wait_ge(u_done, l * 20 + u + 1)
                    if u >= 10:
                        A(V[0:R, tt, c * HG * DV:(c + 1) * HG * DV].rearrange("p (h d) -> p h d", h=HG),
                          ps[0:R, b, :].rearrange("p (h d) -> p h d", h=HG)[:, :, NOPE:], ACT.Copy)
                    if u >= 2:
                        act.wait_ge(u_ss, l * 20 + u - 1)
                    if u < 10:
                        A(s[0:R, 0:HG * QK], ps[0:R, b, 0:HG * QK], ACT.Square).then_inc(u_sq, 1)
                    else:
                        A(s[0:R, 0:HG * NOPE].rearrange("p (h d) -> p h d", h=HG),
                          ps[0:R, b, :].rearrange("p (h d) -> p h d", h=HG)[:, :, 0:NOPE],
                          ACT.Square).then_inc(u_sq, 1)

                def unit_root(u):
                    tt = u % NT
                    R = TA[tt][1]
                    act.wait_ge(u_ss, l * 20 + u + 1)
                    if u < 10:
                        A(ust[0:R, u, :], uss[0:R, u % 3, :], ACT.Sqrt, bias=C("eps_q", R),
                          scale=1.0).then_inc(u_std, 1)
                    else:
                        A(ust[0:R, u, :], uss[0:R, u % 3, :], ACT.Sqrt, bias=small[0:R, 8 + tt:9 + tt],
                          scale=1.0 / QK).then_inc(u_std, 1)

                def unit_read(u):
                    b = AUX_BANK[("tr", u)]
                    c, tt = u // NT % 2, u % NT
                    t0, R = TA[tt]
                    act.wait_ge(tr_done, l * 20 + u + 1)
                    dst, g = (qT, "qh_g") if u < 10 else (kT, "kh_g")
                    A(dst[0:QK, c * HG:(c + 1) * HG, t0:t0 + R],
                      ps[0:QK, b, :].rearrange("p (h t) -> p h t", h=HG)[:, :, 0:R], ACT.Copy,
                      scale=PAR(g, 0, QK)).then_inc(tr_read, 1)

                def conv_hi(f):
                    act.wait_ge(yc_new, l * 2 + f + 1)
                    A(yh[:, f, :], btile[f][:, :], ACT.Copy).then_inc(yc_hi, 1)

                for n in range(N_IN - 1):
                    if n == 0:
                        root(2 * l + 1)
                    if n <= 2:
                        src = raw[:, n, :] if n < 2 else ckv[:, :]
                        act.wait_ge(raw_new, l * 4 + n + 1)
                        if n == 1:
                            act.wait_ge(tabs_new, l + 1)
                        A(lat_sq[n][:, :], src, ACT.Square).then_inc(raw_sq, 1)
                    if n == 4:
                        for i in LOADS[n]:
                            hi(l, i)
                        for i, (b, s, d) in enumerate(((6, Q_LORA, tmp), (4, KV_LORA, sq0))):
                            act.wait_ge(raw_ms, l * 2 + 2)
                            A(two(d[:, :]), pair(b), ACT.Sqrt, bias=C("eps"), scale=1.0 / s).then_inc(lat_std, 1)
                        for k in range(3):
                            act.wait_ge(lat_new, l * 3 + k + 1)
                            A(ch[:, k, :], [raw[:, 0, :], raw[:, 1, :], ckv[:, :]][k], ACT.Copy).then_inc(lat_hi, 1)
                    items = GAPS.get(n, [])
                    for kind, i in items:
                        if kind == "tr":
                            unit_read(i)
                    us = [i for kind, i in items if kind == "u"]
                    for i in us[:2]:
                        unit(i)
                    for j, i in enumerate(us):
                        unit_root(i)
                        if j == 0 and len(us) == 3:
                            unit(us[2])
                    if n == 16:
                        conv_hi(0)
                    if n == 15:
                        for f in range(2):
                            act.wait_ge(gz_new, l * 4 + 3 + f)
                            A(gate[:, f, :], gate[:, f, :], ACT.Silu).then_inc(gate_new, 1)
                    if n != 4:
                        for i in LOADS[n]:
                            hi(l, i)

                for h in range(RH):
                    if h >= 2:
                        act.wait_ge(ro_done, l * 4 + h - 1)
                    act.wait_ge(rs_done, l * 12 + 3 * h + 1)
                    A(two(sc(h, 0, P, 0, T)), pair(4), ACT.Copy).then_inc(rs_read, 1)
                    act.wait_ge(rs_done, l * 12 + 3 * h + 2)
                    A(sc(h, 1, P, 0, T - P), ps[:, 6, 0:T - P], ACT.Copy).then_inc(rs_read, 1)
                    if h == 0:
                        conv_hi(1)
                        for i in LOADS[N_IN - 1]:
                            hi(l, i)

                for u in range(40):
                    q0, R = TA[query(u // NH)]
                    L = q0 + R
                    b = s_bank(u)
                    act.wait_ge(a_max, l * 40 + u + 1)
                    if u >= 3:
                        act.wait_ge(a_tr, l * 40 + u - 2)
                    A(pb[0:R, u % 3, 0:L], psf[0:R, b * 512:b * 512 + L], ACT.Exp,
                      bias=nmax[0:R, u:u + 1], accum_out=esum[0:R, u:u + 1]).then_inc(a_exp, 1)
                    if u % 2 == 0 and 2 <= u <= 32:
                        pt_read(act, A, l, u - 1)
                    if u % NH == 5 and u > NH:
                        y_hi(act, A, l, u // NH - 1)
                act.wait_ge(ro_ss, l + 1)
                A(small[:, 32:52], small[:, 52:72], ACT.Sqrt, bias=C("eps"), scale=1.0 / RD).then_inc(ro_std, 1)
                y_hi(act, A, l, NT - 1)
                for f in range(2):
                    act.wait_ge(yr_new, l * 2 + f + 1)
                    A(yh[:, 2 + f, :], gate[:, f, :], ACT.Copy).then_inc(yr_hi, 1)

                for n in range(N_IN, PRE_TILES):
                    x_split("mlp_g", n - N_IN, xm_new, xm_hi, l * KT + n - N_IN + 1)
                    if n in LOADS:
                        for i in LOADS[n]:
                            hi(l, i)
                    else:
                        mlp_hi(l, 0, n - 22, tile_no(l, n))

                group(l, 0, "first")
                with act.Fori(1, NGRP - 1) as g:
                    group(l, g, "middle")
                group(l, NGRP - 1, "last")

            for i in range(1, 8, 2):
                act.wait_ge(fin_tr, i + 1)
                t, f = i // 2, i % 2
                act.wait_ge(fin_read, i)
                A(xout[:, t, f * 512:(f + 1) * 512], ps[:, i % 4, :], ACT.Copy).then_inc(fin_read, 1)

        @block.vector
        def _(dve):
            TT = nc.vector.tensor_tensor
            TS = nc.vector.tensor_scalar
            STT = nc.vector.scalar_tensor_tensor
            copy = nc.vector.tensor_copy
            drain = nc.vector.drain
            dve.sem_inc(t_read, L_TILES)
            dve.sem_inc(w_lo, W_PRIME)
            nc.vector.memset(small[:, :], 1.0)
            dve.wait_ge(par_in, 16)

            def x_low(g, k, sem_hi, sem_lo, value):
                dve.wait_ge(sem_hi, value)
                STT(hl[:, k, :], xT[:, k, :], PAR(g, k), hh[:, k, :].bitcast(F32), ALU.mult,
                    ALU.subtract).then_inc(sem_lo, 1)


            def source(i):
                st = stage[:, (i // 2) % SS, :]
                h = i % 2
                if HALVES[i] == ("T", 2):
                    return st[:, 0:KT * 160].rearrange("p (k n) -> p k n", k=KT)[:, :, 0:P], KT
                if HALVES[i] == ("T", 3):
                    return st[:, 0:KT * 160].rearrange("p (k n) -> p k n", k=KT)[:, :, 32:160], KT
                if HALVES[i][0] == "T":
                    return st.rearrange("p (k n) -> p k n", k=KT)[:, :, h * P:(h + 1) * P], KT
                w = HG * QK if HALVES[i][1] < 4 else 512
                return st[:, h * w:(h + 1) * w], w

            def low(l, i):
                dve.wait_ge(w_hi, half_no(l, i))
                src, n = source(i)
                s = SLOT[i]
                if n == KT:
                    h, o = (w[:, s, :].rearrange("p (k n) -> p k n", k=KT) for w in (wh, wl))
                else:
                    h, o = (w[:, s, 0:n] for w in (wh, wl))
                TT(o, src, h.bitcast(F32), ALU.subtract).then_inc(w_lo, 1)

            def mlp_low(l, g, m):
                dve.wait_ge(w_hi, l * L_HALVES + PRE_HALVES + g * GT + m + 1)
                h, o = (w[:, m % WS, :].rearrange("p (k n) -> p k n", k=KT) for w in (wh, wl))
                src = stage[:, (m // 2) % SS, :].rearrange("p (k n) -> p k n", k=KT)
                TT(o, src[:, :, (m % 2) * P:(m % 2 + 1) * P], h.bitcast(F32), ALU.subtract).then_inc(w_lo, 1)

            def invert(value):
                dve.wait_ge(std_new, value)
                nc.vector.reciprocal(rstd[:, :], tmp[:, :])
                drain()

            def x_add(k, no, value, done):
                dve.wait_ge(t_done, value)
                TT(two(xT[:, k, :]), pair(2 * (no % 2)), two(xT[:, k, :]), ALU.add).then_inc(t_read, 1)
                drain()
                if done is not None:
                    dve.sem_inc(done, 1)

            def group(l, g, kind):
                for m in range(GT):
                    value = (l + 1) * L_TILES + PRE_TILES + g * GT + m + 1
                    if m < 8:
                        if kind == "first" and m == 0:
                            invert(2 * l + 2)
                        dve.wait_ge(t_done, value)
                        TT(two(tb[:, m % 2, :]), pair(2 * (m % 2)), two(rstd[:, :]), ALU.mult).then_inc(t_read, 1)
                        drain()
                        STT(ts[:, m % 2, :], tb[:, m % 2, :], 0.0, tb[:, m % 2, :], ALU.max,
                            ALU.mult).then_inc(s_new, 1)
                    else:
                        x_add(m - 8, m, value, xa_new if kind == "last" else None)
                    if kind != "last" or m < GT - 4:
                        mlp_low(l, g if m < GT - 4 else g + 1, (m + 4) % GT)
                    else:
                        low(l + 1, m - (GT - 4))
                    if m < 8:
                        dve.wait_ge(s_hi, (l * NGRP + g) * 8 + m + 1)
                        TT(yl[:, m, :], ts[:, m % 2, :], yh[:, m, :].bitcast(F32), ALU.subtract).then_inc(s_lo, 1)
                    elif kind == "last":
                        if m == 8:
                            dve.wait_ge(par_in, 16 * (l + 2))
                        x_low("attn_g", m - 8, xa_hi, xa_lo, (l + 1) * KT + m - 7)

            for k in range(KT):
                b = 2 * (k % 2)
                dve.wait_ge(xt_done, k + 1)
                copy(xT[:, k, 0:META], ps[:, b + 1, 0:META])
                copy(xT[:, k, META:T], ps[:, b, :]).then_inc(xt_read, 1)
                drain()
                dve.sem_inc(xa_new, 1)
                if k:
                    x_low("attn_g", k - 1, xa_hi, xa_lo, k)
                if k == KT - 1:
                    low(0, 0)
            x_low("attn_g", KT - 1, xa_hi, xa_lo, KT)
            for i in range(1, 4):
                low(0, i)
            dve.wait_ge(ident_in, 16)
            dve.wait_ge(con_in, 32)
            copy(identb[:, :], ident)
            copy(maskb[:, :], mneg[:, :])
            with dve.Fori(0, DEPTH) as l:
                def unit_sum(u):
                    R = TA[u % NT][1]
                    w = QK if u < 10 else NOPE
                    dve.wait_ge(u_sq, l * 20 + u + 1)
                    if u >= 3:
                        dve.wait_ge(u_std, l * 20 + u - 2)
                    nc.vector.tensor_reduce(
                        uss[0:R, u % 3, :], [sq0, sq1][u % 2][0:R, 0:HG * w].rearrange("p (h d) -> p h d", h=HG),
                        AX, ALU.add).then_inc(u_ss, 1)

                def unit_norm(u):
                    b = AUX_BANK[("u", u)]
                    tt = u % NT
                    R = TA[tt][1]
                    dve.wait_ge(u_std, l * 20 + u + 1)
                    nc.vector.reciprocal(ust[0:R, u, :], ust[0:R, u, :])
                    drain()
                    if u >= 3:
                        dve.wait_ge(tr_done, l * 20 + u - 2)
                    o = qn[0:R, u % 3, :].rearrange("p (h d) -> p h d", h=HG)
                    r = ust[0:R, u, :].unsqueeze(2)
                    if u < 10:
                        TT(o, ps[0:R, b, 0:HG * QK].rearrange("p (h d) -> p h d", h=HG),
                           r.broadcast_to([R, HG, QK]), ALU.mult).then_inc(u_read, 1)
                        drain()
                        HR = ROPE // 2
                        tc, tsn = (rt[0:R, i, :].rearrange("p (h d) -> p h d", h=HG) for i in range(2))

                        def tab(i, a, c):
                            return tabs[0:R, i, tt, a:c].unsqueeze(1).broadcast_to([R, HG, c - a])

                        TT(tc, o[:, :, NOPE:QK], tab(0, 0, ROPE), ALU.mult)
                        TT(tsn[:, :, 0:HR], o[:, :, NOPE + HR:QK], tab(1, 0, HR), ALU.mult)
                        TT(tsn[:, :, HR:ROPE], o[:, :, NOPE:NOPE + HR], tab(1, HR, ROPE), ALU.mult)
                        drain()
                        TT(o[:, :, NOPE:QK], tc, tsn, ALU.add).then_inc(u_tok, 1)
                    else:
                        TT(o[:, :, 0:NOPE], ps[0:R, b, :].rearrange("p (h d) -> p h d", h=HG)[:, :, 0:NOPE],
                           r.broadcast_to([R, HG, NOPE]), ALU.mult).then_inc(u_read, 1)
                        TT(o[:, :, NOPE:QK], krg[0:R, tt, :].unsqueeze(1).broadcast_to([R, HG, ROPE]),
                           r.broadcast_to([R, HG, ROPE]), ALU.mult)
                        drain()
                        dve.sem_inc(u_tok, 1)

                def scaled(n, dst, rows=slice(0, P)):
                    dve.wait_ge(t_done, tile_no(l, n))
                    b = 2 * (n % 2)
                    return TT(two(dst), ps[rows, b:b + 2, 0:TH], two(rstd[rows, :]), ALU.mult)

                def rope(i):
                    dve.wait_ge(rp_done, l * 4 + i + 1)
                    TT(two(tmp[:, :]), pair(4 + 2 * (i % 2)), two(C("rope_s")), ALU.mult)
                    TT(rqk[:, i, :], rqk[:, i, :], C("rope_c"), ALU.mult)
                    drain()
                    TT(rqk[:, i, :], rqk[:, i, :], tmp[:, :], ALU.add)
                    drain()
                    dve.sem_inc(rp_read, 1)

                def conv_out(f):
                    TT(btile[f][:, :], btile[f][:, :], cacc[f][:, :], ALU.mult).then_inc(yc_new, 1)

                def conv_low(f):
                    dve.wait_ge(yc_hi, l * 2 + f + 1)
                    TT(yl[:, f, :], btile[f][:, :], yh[:, f, :].bitcast(F32), ALU.subtract).then_inc(yc_lo, 1)

                def freed():
                    drain()
                    dve.sem_inc(t_read, 1)

                def rope_tables():
                    for i, (g, t) in enumerate((("qrope_g", "tok_c"), ("qrope_g", "tok_s"), ("krope_g", "tok_c"),
                                                ("krope_g", "tok_s"))):
                        o = PARAMS[g][0]
                        t3 = C(t).rearrange("p (t d) -> p t d", t=NT)
                        if i % 2 == 0:
                            TT(tabs[:, i, :, :], t3, par[:, o:o + ROPE].unsqueeze(1).broadcast_to([P, NT, ROPE]),
                               ALU.mult)
                        else:
                            HR = ROPE // 2
                            for a, c in ((0, HR), (HR, 0)):
                                TT(tabs[:, i, :, a:a + HR], t3[:, :, a:a + HR],
                                   par[:, o + c:o + c + HR].unsqueeze(1).broadcast_to([P, NT, HR]), ALU.mult)

                rope_tables()
                invert(2 * l + 1)
                dve.sem_inc(tabs_new, 1)
                for n in range(N_IN - 1):
                    if n < 2:
                        scaled(n, raw[:, n, :])
                    elif n == 2:
                        scaled(n, ckv[:, :])
                    elif n == 3:
                        scaled(n, krT[96:P, :], slice(96, P))
                    elif n < 8:
                        scaled(n, rqk[:, n - 4, :])
                    elif n < 10:
                        scaled(n, raw[:, n - 8, :])
                    elif n < 12:
                        scaled(n, gate[:, n - 10, :])
                    elif n < 14:
                        scaled(n, cu[n - 12][:, :])
                    elif n < 16:
                        scaled(n, sq0[:, :])
                    else:
                        scaled(n, btile[0][:, :])
                    freed()
                    if n < 4:
                        dve.sem_inc(raw_new, 1)
                    if 4 <= n < 8:
                        dve.sem_inc(rq_new, 1)
                    if 8 <= n < 12:
                        dve.sem_inc(gz_new, 1)
                    if n == 15:
                        rope(2)
                        rope(3)
                    if n in (14, 15):
                        f = n - 14
                        TT(cu[f][:, :], cu[f][:, :], sq0[:, :], ALU.mult)
                        drain()
                        TS(cacc[f][:, :], cu[f][:, :], PAR("conv", 3 * f + 2), None, ALU.mult)
                        drain()
                        STT(cacc[f][:, 1:T], cu[f][:, 0:T - 1], PAR("conv", 3 * f + 1), cacc[f][:, 1:T],
                            ALU.mult, ALU.add)
                        drain()
                        STT(cacc[f][:, 2:T], cu[f][:, 0:T - 2], PAR("conv", 3 * f), cacc[f][:, 2:T],
                            ALU.mult, ALU.add)
                    if n == 4:
                        for i in LOADS[n]:
                            low(l, i)
                        for i, (s, d, ks) in enumerate(((tmp, acc, (0, 1)), (sq0, tmp, (2,)))):
                            dve.wait_ge(lat_std, l * 2 + 1 + i)
                            nc.vector.reciprocal(d[:, :], s[:, :])
                            drain()
                            for k in ks:
                                src = [raw[:, 0, :], raw[:, 1, :], ckv[:, :]][k]
                                g = PAR("qn_g", k) if k < 2 else PAR("kvn_g")
                                STT(src, src, g, d[:, :], ALU.mult, ALU.mult).then_inc(lat_new, 1)
                        for k in range(3):
                            dve.wait_ge(lat_hi, l * 3 + k + 1)
                            TT(cl[:, k, :], [raw[:, 0, :], raw[:, 1, :], ckv[:, :]][k], ch[:, k, :].bitcast(F32),
                               ALU.subtract).then_inc(lat_lo, 1)
                    if n == 5:
                        nc.vector.memset(kr[:, 0, :], 0.0)
                        drain()
                        dve.wait_ge(kr_tr, l + 1)
                        copy(kr[0:META, 0, :], ps[0:META, 6, 0:ROPE])
                        copy(kr[:, 1:NT, :], ps[:, 6, ROPE:NT * ROPE].rearrange("p (t d) -> p t d", d=ROPE))
                        drain()
                        dve.sem_inc(kr_read, 1)
                        HR = ROPE // 2
                        t1 = sq0[:, 0:NT * ROPE].rearrange("p (t d) -> p t d", t=NT)
                        t2 = tmp[:, 0:NT * ROPE].rearrange("p (t d) -> p t d", t=NT)
                        TT(t2, kr[:, :, :], kr[:, :, :], ALU.mult)
                        TT(krg[:, :, :], kr[:, :, :], tabs[:, 2, :, :], ALU.mult)
                        TT(t1[:, :, 0:HR], kr[:, :, HR:ROPE], tabs[:, 3, :, 0:HR], ALU.mult)
                        TT(t1[:, :, HR:ROPE], kr[:, :, 0:HR], tabs[:, 3, :, HR:ROPE], ALU.mult)
                        drain()
                        TT(krg[:, :, :], krg[:, :, :], t1, ALU.add)
                        nc.vector.tensor_reduce(small[:, 8:8 + NT], t2, AX, ALU.add)
                        drain()
                        TS(small[:, 8:8 + NT], small[:, 8:8 + NT], 1.0 / QK, EPS, ALU.mult, ALU.add)
                        drain()
                        dve.sem_inc(kr_ss, 1)
                    us = [i for kind, i in GAPS.get(n, []) if kind == "u"]
                    for i in us:
                        unit_sum(i)
                    for i in us:
                        unit_norm(i)
                    if n == 14:
                        rope(0)
                        rope(1)
                    if n == 16:
                        dve.wait_ge(rv_tr, l + 1)
                        for it, (t0, R) in enumerate(TB):
                            o = (it % 2) * 256
                            gi = CONSTS["g_in"][0] + it * RH
                            TT(vtok[0:R, it, :].rearrange("p (h d) -> p h d", h=RH),
                               ps[0:R, 4 + it // 2, o:o + 256].rearrange("p (h d) -> p h d", h=RH),
                               con[0:R, gi:gi + RH].unsqueeze(2).broadcast_to([R, RH, RD]), ALU.mult)
                        drain()
                        dve.sem_inc(rv_read, 1)
                    if n == 16:
                        conv_out(0)
                    if n != 4:
                        for i in LOADS[n]:
                            low(l, i)
                    if n == 16:
                        conv_low(0)

                def heads(ap, r, a, b, pair_no):
                    return ap[0:r, a:b, :].rearrange("p t (h d) -> p t h d", h=RH)[:, :, 2 * pair_no:2 * pair_no + 2, :]

                squares = (pt, sc_odd[:, 0:1024].rearrange("p (a c) -> p a c", a=2))
                parts = ((P, 0, NT - 1), (TB[-1][1], NT - 1, NT))

                def ret_out(c, i):
                    dve.wait_ge(ro_done, l * 4 + 2 * c + 2)
                    o = CONSTS["g_out"][0]
                    decay = con[:, o:o + NT * RH].rearrange("p (t h) -> p t h", t=NT)
                    r, a, b = parts[i]
                    TT(heads(ort, r, a, b, c),
                       ps[0:r, 2 * c + i, 0:(b - a) * P].rearrange("p (t h d) -> p t h d", h=2, d=RD),
                       decay[0:r, a:b, 2 * c:2 * c + 2].unsqueeze(3).broadcast_to([r, b - a, 2, RD]),
                       ALU.mult).then_inc(ro_read, 1)

                def ret_squares(c):
                    for i, (r, a, b) in enumerate(parts):
                        sq = squares[c][0:r, i, 0:(b - a) * P].rearrange("p (t h d) -> p t h d", h=2, d=RD)
                        TT(sq, heads(ort, r, a, b, c), heads(ort, r, a, b, c), ALU.mult)
                    drain()
                    ss = small[:, 52:72].rearrange("p (t h) -> p t h", t=NT)
                    for i, (r, a, b) in enumerate(parts):
                        sq = squares[c][0:r, i, 0:(b - a) * P].rearrange("p (t h d) -> p t h d", h=2, d=RD)
                        nc.vector.tensor_reduce(ss[0:r, a:b, 2 * c:2 * c + 2], sq, AX, ALU.add)

                def ret_diag(h):
                    for j in (0, 1):
                        dve.wait_ge(rs_read, l * 8 + 2 * h + j + 1)
                        s = sc(h, j, P, 0, P)
                        TT(s, s, C("keep"), ALU.mult).then_inc(rs_diag, 1)
                    dve.wait_ge(rs_done, l * 12 + 3 * h + 3)
                    for j in (2, 3, 4):
                        R = TB[j][1]
                        n, c = T - TB[j][0], SC_OFF[j] - SC_OFF[2]
                        TT(sc(h, j, R, 0, R), ps[0:R, 7, c:c + R], C("keep", R)[:, 0:R],
                           ALU.mult).then_inc(rs_diag, 1)
                        if n > R:
                            copy(sc(h, j, P, R, n), ps[:, 7, c + R:c + n]).then_inc(rs_diag, 1)

                ret_diag(0)
                scaled(N_IN - 1, btile[1][:, :])
                freed()
                conv_out(1)
                for i in LOADS[N_IN - 1]:
                    low(l, i)
                conv_low(1)
                ret_diag(1)
                ret_diag(2)
                ret_out(0, 0)
                ret_out(0, 1)
                drain()
                ret_squares(0)
                ret_diag(3)
                def biggest(u):
                    q0, R = TA[query(u // NH)]
                    b = s_bank(u)
                    dve.wait_ge(a_s, l * 40 + u + 1)
                    nc.vector.tensor_reduce(nmax[0:R, u:u + 1], psf[0:R, b * 512:b * 512 + q0 + R], AX, ALU.max,
                                            negate=True).then_inc(a_max, 1)

                def ptm_read(u):
                    R = TA[query(u // NH)][1]
                    dve.wait_ge(a_tr, l * 40 + u + 1)
                    if u >= 2:
                        dve.wait_ge(a_pv, l * 40 + u - 1)
                    copy(ptm[0:META, u % 2, 0:R], meta_keys(u)).then_inc(a_ptm, 1)

                def normalised(turn):
                    R = TA[query(turn)][1]
                    dve.wait_ge(a_pv, l * 40 + turn * NH + NH)
                    nc.vector.reciprocal(esum[0:R, turn * NH:(turn + 1) * NH], esum[0:R, turn * NH:(turn + 1) * NH])
                    drain()
                    if turn:
                        dve.wait_ge(a_ytr, l * NT + turn)
                    TT(yo[0:R, :].rearrange("p (h d) -> p h d", h=NH),
                       ps[0:R, o_bank(turn), :].rearrange("p (h d) -> p h d", h=NH),
                       esum[0:R, turn * NH:(turn + 1) * NH].unsqueeze(2).broadcast_to([R, NH, DV]),
                       ALU.mult).then_inc(a_o, 1)

                def y_low(turn):
                    t0, R = TA[query(turn)]
                    dve.wait_ge(ya_hi, l * NT + turn + 1)
                    TT(yl[:, 4:8, t0:t0 + R], ps[:, o_bank(turn), :].rearrange("p (f t) -> p f t", f=4)[:, :, 0:R],
                       yh[:, 4:8, t0:t0 + R].bitcast(F32), ALU.subtract).then_inc(ya_lo, 1)

                def ret_norm():
                    dve.wait_ge(ro_std, l + 1)
                    nc.vector.reciprocal(small[:, 32:52], small[:, 32:52])
                    drain()
                    scale = small[:, 32:52].rearrange("p (t h) -> p t h", t=NT)
                    for r, a, b in parts:
                        o = ort[0:r, a:b, :].rearrange("p t (h d) -> p t h d", h=RH)
                        TT(o, o, scale[0:r, a:b, :].unsqueeze(3).broadcast_to([r, b - a, RH, RD]), ALU.mult)
                    drain()
                    dve.sem_inc(ro_tok, 1)

                def ret_gate(f):
                    dve.wait_ge(gate_new, l * 2 + 2)
                    dve.wait_ge(ry_tr, l * 2 + f + 1)
                    o = (4 + 2 * f) * 512
                    STT(gate[:, f, :], psf[:, o:o + T], PAR("ret_g", f), gate[:, f, :], ALU.mult,
                        ALU.mult).then_inc(yr_new, 1)

                def ret_low(f):
                    dve.wait_ge(yr_hi, l * 2 + f + 1)
                    TT(yl[:, 2 + f, :], gate[:, f, :], yh[:, 2 + f, :].bitcast(F32), ALU.subtract).then_inc(yr_lo, 1)

                biggest(0)
                biggest(1)
                ret_out(1, 1)
                for u in range(2, 41):
                    if u == 2:
                        pt_read(dve, None, l, 0)
                        ptm_read(0)
                    if u < 40:
                        biggest(u)
                    if u == 6:
                        ret_out(1, 0)
                    if u == 11:
                        ret_squares(1)
                        drain()
                        dve.sem_inc(ro_ss, 1)
                    if u >= 1:
                        v = u - 1
                        if v < 32 and v % 2 == 0:
                            pt_read(dve, None, l, v)
                        ptm_read(v)
                    if u % NH == 1 and u > NH:
                        normalised(u // NH - 1)
                    if u % NH == 6 and u > NH:
                        y_low(u // NH - 1)
                normalised(NT - 1)
                ret_norm()
                y_low(NT - 1)
                for f in range(2):
                    ret_gate(f)
                for f in range(2):
                    ret_low(f)

                for n in range(N_IN, PRE_TILES):
                    k = n - N_IN
                    x_add(k, n, tile_no(l, n), xm_new)
                    if n in LOADS:
                        for i in LOADS[n]:
                            low(l, i)
                    else:
                        mlp_low(l, 0, n - 22)
                    x_low("mlp_g", k, xm_hi, xm_lo, l * KT + k + 1)

                group(l, 0, "first")
                with dve.Fori(1, NGRP - 1) as g:
                    group(l, g, "middle")
                group(l, NGRP - 1, "last")

            for i in range(0, 8, 2):
                dve.wait_ge(fin_tr, i + 1)
                if i:
                    dve.wait_ge(fin_read, i)
                copy(xout[:, i // 2, 0:512], ps[:, i % 4, :]).then_inc(fin_read, 1)

        @block.gpsimd
        def _(pool):
            def squares(sem_new, value, sem_sq, reads):
                for k in range(KT):
                    pool.wait_ge(sem_new, value + k + 1)
                    if k == 0:
                        if reads is not None:
                            pool.wait_ge(ms_done, reads)
                        nc.gpsimd.tensor_tensor(acc[:, :], xT[:, 0, :], xT[:, 0, :], ALU.mult)
                        continue
                    nc.gpsimd.tensor_tensor(sqx[:, :], xT[:, k, :], xT[:, k, :], ALU.mult)
                    nc.gpsimd.drain()
                    last = nc.gpsimd.tensor_tensor(acc[:, :], acc[:, :], sqx[:, :], ALU.add)
                    if k < KT - 1:
                        nc.gpsimd.drain()
                last.then_inc(sem_sq, 1)

            squares(xa_new, 0, xa_sq, None)
            with pool.Fori(0, DEPTH) as l:
                squares(xm_new, l * KT, xm_sq, 2 * l + 1)
                squares(xa_new, (l + 1) * KT, xa_sq, 2 * l + 2)


def constants():
    import numpy as np
    f = np.float32
    c = np.zeros((P, N_CONST), f)

    def put(name, a):
        o, w = CONSTS[name]
        c[:, o:o + w] = a

    p = np.arange(P)
    put("ident", np.eye(P, dtype=f))
    put("perm", (p[:, None] == (p ^ 32)[None, :]).astype(f))
    put("ones", 1.0)
    put("keep", (p[None, :] >= p[:, None]).astype(f))

    def angles(dim):
        inv = f(1.0) / (f(10000.0) ** (np.arange(0, dim, 2, dtype=f) / f(dim)))
        ang = np.arange(T, dtype=f)[:, None] * inv[None, :]
        return np.cos(ang).astype(f), np.sin(ang).astype(f)

    cr, sr = angles(RD)
    half = RD // 2
    put("rope_c", cr.T[p % half])
    put("rope_s", sr.T[p % half] * np.where(p % RD < half, -1, 1)[:, None])
    cm, sm = angles(ROPE)
    tc, ts = np.zeros((P, NT, ROPE), f), np.zeros((P, NT, ROPE), f)
    for t, (t0, n) in enumerate(TA):
        tc[:n, t] = np.concatenate([cm[t0:t0 + n], cm[t0:t0 + n]], 1)
        ts[:n, t] = np.concatenate([-sm[t0:t0 + n], sm[t0:t0 + n]], 1)
    put("tok_c", tc.reshape(P, -1))
    put("tok_s", ts.reshape(P, -1))
    log_g = np.log1p(-np.exp2(-5.0 - np.arange(RH)))
    pos = (p[:, None] + P * np.arange(NT)[None, :])[:, :, None] * log_g
    put("g_out", np.exp(pos).reshape(P, -1))
    put("g_in", (np.exp(-pos) * RD ** -0.5).reshape(P, -1))
    put("eps", EPS)
    put("eps_q", QK * EPS)
    mask = np.where(p[None, :] <= p[:, None], 0.0, NEG).astype(f)
    return c, mask


def kernel(x, meta_tokens, attn_norm_g, w_in, conv_w, ret_gn_g, q_norm_g, w_uq, kv_norm_g, w_ukv,
           q_head_norm_g, k_head_norm_g, w_out, mlp_norm_g, w_mlp_in, w_mlp_out):
    import numpy as np
    import concourse.bacc as bacc
    from concourse.bass_utils import run_bass_kernel_spmd as run

    con, mask = constants()
    par = np.ones((DEPTH + 1, P, N_PARAM), np.float32)

    def put(name, a):
        o, w = PARAMS[name]
        par[:DEPTH, :a.shape[1], o:o + w] = a

    put("attn_g", np.asarray(attn_norm_g).reshape(DEPTH, KT, P).transpose(0, 2, 1))
    put("mlp_g", np.asarray(mlp_norm_g).reshape(DEPTH, KT, P).transpose(0, 2, 1))
    put("qn_g", np.asarray(q_norm_g).reshape(DEPTH, 2, P).transpose(0, 2, 1))
    put("kvn_g", np.asarray(kv_norm_g).reshape(DEPTH, P, 1))
    put("conv", np.asarray(conv_w).reshape(DEPTH, 3, 2, P).transpose(0, 3, 2, 1).reshape(DEPTH, P, 6))
    put("ret_g", np.asarray(ret_gn_g).reshape(DEPTH, 2, P).transpose(0, 2, 1))
    put("qh_g", np.asarray(q_head_norm_g)[:, :NOPE, None])
    put("kh_g", np.asarray(k_head_norm_g)[:, :NOPE, None])
    put("qrope_g", np.broadcast_to(np.asarray(q_head_norm_g)[:, None, NOPE:], (DEPTH, P, ROPE)))
    put("krope_g", np.broadcast_to(np.asarray(k_head_norm_g)[:, None, NOPE:], (DEPTH, P, ROPE)))
    par[DEPTH] = par[DEPTH - 1]

    nc = bacc.Bacc("TRN2", target_bir_lowering=False, num_devices=1)
    arrays = {"x": x, "meta": meta_tokens, "consts": con, "maskneg": mask, "params": par, "w_in": w_in,
              "w_uq": w_uq, "w_ukv": w_ukv, "w_out": w_out, "w_mlp_in": w_mlp_in, "w_mlp_out": w_mlp_out}
    arrays = {f"{n}_dram": np.ascontiguousarray(a) for n, a in arrays.items()}
    args = [nc.dram_tensor(n, a.shape, mybir.dt.from_np(a.dtype), kind="ExternalInput").ap()
            for n, a in arrays.items()]
    out = nc.dram_tensor("out_dram", (1, SEQ, D), F32, kind="ExternalOutput").ap()
    trunk(nc, *args, out)
    return run(nc, [arrays], core_ids=[0]).results[0]["out_dram"]
```
